# Optimizing a Trainium2 kernel written in Bass

```python
import jax, jax.numpy as jnp
from jax import lax
import numpy as np
import math

D_MODEL = 1024
BATCH = 1
SEQ = 256
DEPTH = 2

N_MIXERS = 2
SB_HEADS = 16
SB_HEAD_DIM = D_MODEL // SB_HEADS
Q_BLOCK = 128
D_RNN = (D_MODEL * 5) // 4
LRU_BLOCKS = 10
LRU_BLOCK_W = D_RNN // LRU_BLOCKS
CONV_W = 4
LRU_C = 8.0
D_FF = ((8 * D_MODEL // 3 + 127) // 128) * 128
N_SUB = 3
MACARON_W = 0.5
EPS = 1e-6
N_SB_LAYERS = (DEPTH + 1) // 2
N_LRU_LAYERS = DEPTH // 2


def rmsnorm(x, g):
    xf = x.astype(jnp.float32)
    inv = lax.rsqrt(jnp.mean(xf * xf, axis=-1, keepdims=True) + EPS)
    return (xf * inv).astype(x.dtype) * g

def sublayer_input(x, g, mod_j):
    shift, scale, gate = mod_j[:, 0], mod_j[:, 1], mod_j[:, 2]
    h = rmsnorm(x, g) * (1 + scale[:, None, :]) + shift[:, None, :]
    return h, (1 + gate)[:, None, :]

def swiglu(h, w_gu, w_down):
    g, u = jnp.split(h @ w_gu, 2, axis=-1)
    return (jax.nn.silu(g) * u) @ w_down

def stick_breaking_attention(h, w_qkv, w_o):
    B, S, _ = h.shape
    qkv = (h @ w_qkv).reshape(B, S, 3, SB_HEADS, SB_HEAD_DIM)
    qkv = jnp.transpose(qkv, (2, 0, 3, 1, 4)).astype(jnp.float32)
    q = qkv[0] * (SB_HEAD_DIM ** -0.5)
    k, v = qkv[1], qkv[2]
    outs = []
    for blk in range(S // Q_BLOCK):
        t0 = blk * Q_BLOCK
        L = t0 + Q_BLOCK
        z = jnp.einsum('bhqd,bhkd->bhqk', q[:, :, t0:L], k[:, :, :L])
        t_idx = t0 + jnp.arange(Q_BLOCK)
        s_idx = jnp.arange(L)
        mask = s_idx[None, :] < t_idx[:, None]
        log_keep = jnp.where(mask, jax.nn.log_sigmoid(-z), 0.0)
        later = lax.cumsum(log_keep, axis=3, reverse=True) - log_keep
        w = jnp.where(mask, jnp.exp(jax.nn.log_sigmoid(z) + later), 0.0)
        outs.append(jnp.einsum('bhqk,bhkd->bhqd', w, v[:, :, :L]))
    o = jnp.concatenate(outs, axis=2)
    o = jnp.transpose(o, (0, 2, 1, 3)).reshape(B, S, D_MODEL).astype(h.dtype)
    return o @ w_o

def _lin_rec_combine(left, right):
    a1, b1 = left
    a2, b2 = right
    return a1 * a2, a2 * b1 + b2

def rglru_block(h, w_in, conv_w, conv_b, w_r, b_r, w_i, b_i, lam, w_out):
    B, S, _ = h.shape
    gate, xb = jnp.split(h @ w_in, 2, axis=-1)
    xp = jnp.pad(xb, ((0, 0), (CONV_W - 1, 0), (0, 0)))
    xc = conv_b + xp[:, 0:S] * conv_w[0]
    for tap in range(1, CONV_W):
        xc = xc + xp[:, tap:tap + S] * conv_w[tap]
    xblk = xc.reshape(B, S, LRU_BLOCKS, LRU_BLOCK_W)
    r = jax.nn.sigmoid(jnp.einsum('bsnk,nkj->bsnj', xblk, w_r).reshape(B, S, D_RNN) + b_r)
    i = jax.nn.sigmoid(jnp.einsum('bsnk,nkj->bsnj', xblk, w_i).reshape(B, S, D_RNN) + b_i)
    log_a = -LRU_C * r.astype(jnp.float32) * jax.nn.softplus(-lam.astype(jnp.float32))
    a = jnp.exp(log_a)
    b = jnp.sqrt(-jnp.expm1(2.0 * log_a)) * (i * xc).astype(jnp.float32)
    _, hs = lax.associative_scan(_lin_rec_combine, (a, b), axis=1)
    y = jax.nn.gelu(gate) * hs.astype(h.dtype)
    return y @ w_out

def first_inputs(seed: int = 0) -> dict:
    key = jax.random.key(seed)
    ks = jax.random.split(key, 24)
    D = D_MODEL
    f32 = jnp.float32
    nrm = lambda k, shape, s: jax.random.normal(k, shape, f32) * s
    x = nrm(ks[0], (BATCH, SEQ, D), 1.0)
    c = nrm(ks[1], (BATCH, D), 1.0)
    mod_w = nrm(ks[2], (DEPTH, D, N_SUB * 3 * D), 0.2 * D ** -0.5)
    mod_b = nrm(ks[3], (DEPTH, N_SUB * 3 * D), 0.05)
    norm_g = 1.0 + nrm(ks[4], (DEPTH, N_SUB, D), 0.02)
    ffn_w_gu = nrm(ks[5], (DEPTH, 2, D, 2 * D_FF), D ** -0.5)
    ffn_w_down = nrm(ks[6], (DEPTH, 2, D_FF, D), D_FF ** -0.5)
    sb_w_qkv = nrm(ks[7], (N_SB_LAYERS, D, 3 * D), D ** -0.5)
    sb_w_o = nrm(ks[8], (N_SB_LAYERS, D, D), D ** -0.5)
    lru_w_in = nrm(ks[9], (N_LRU_LAYERS, D, 2 * D_RNN), D ** -0.5)
    lru_conv_w = nrm(ks[10], (N_LRU_LAYERS, CONV_W, D_RNN), CONV_W ** -0.5)
    lru_conv_b = nrm(ks[11], (N_LRU_LAYERS, D_RNN), 0.02)
    lru_w_r = nrm(ks[12], (N_LRU_LAYERS, LRU_BLOCKS, LRU_BLOCK_W, LRU_BLOCK_W), LRU_BLOCK_W ** -0.5)
    lru_b_r = nrm(ks[13], (N_LRU_LAYERS, D_RNN), 0.1)
    lru_w_i = nrm(ks[14], (N_LRU_LAYERS, LRU_BLOCKS, LRU_BLOCK_W, LRU_BLOCK_W), LRU_BLOCK_W ** -0.5)
    lru_b_i = nrm(ks[15], (N_LRU_LAYERS, D_RNN), 0.1)
    a_c = jax.random.uniform(ks[16], (N_LRU_LAYERS, D_RNN), f32, 0.9, 0.999)
    a0 = a_c ** (1.0 / LRU_C)
    lru_lambda = jnp.log(a0) - jnp.log1p(-a0)
    lru_w_out = nrm(ks[17], (N_LRU_LAYERS, D_RNN, D), D_RNN ** -0.5)
    final_norm_g = 1.0 + nrm(ks[18], (D,), 0.02)
    return {"x": x, "c": c, "mod_w": mod_w, "mod_b": mod_b, "norm_g": norm_g,
            "ffn_w_gu": ffn_w_gu, "ffn_w_down": ffn_w_down,
            "sb_w_qkv": sb_w_qkv, "sb_w_o": sb_w_o,
            "lru_w_in": lru_w_in, "lru_conv_w": lru_conv_w, "lru_conv_b": lru_conv_b,
            "lru_w_r": lru_w_r, "lru_b_r": lru_b_r, "lru_w_i": lru_w_i, "lru_b_i": lru_b_i,
            "lru_lambda": lru_lambda, "lru_w_out": lru_w_out, "final_norm_g": final_norm_g}

def first_block(x, c, mod_w, mod_b, norm_g, ffn_w_gu, ffn_w_down, sb_w_qkv, sb_w_o,
              lru_w_in, lru_conv_w, lru_conv_b, lru_w_r, lru_b_r, lru_w_i, lru_b_i,
              lru_lambda, lru_w_out, final_norm_g):
    B = x.shape[0]
    c_act = jax.nn.silu(c)
    for layer in range(DEPTH):
        mod = (c_act @ mod_w[layer] + mod_b[layer]).reshape(B, N_SUB, 3, D_MODEL)
        h, g = sublayer_input(x, norm_g[layer, 0], mod[:, 0])
        x = x + MACARON_W * g * swiglu(h, ffn_w_gu[layer, 0], ffn_w_down[layer, 0])
        h, g = sublayer_input(x, norm_g[layer, 1], mod[:, 1])
        j = layer // N_MIXERS
        if layer % N_MIXERS == 0:
            y = stick_breaking_attention(h, sb_w_qkv[j], sb_w_o[j])
        else:
            y = rglru_block(h, lru_w_in[j], lru_conv_w[j], lru_conv_b[j], lru_w_r[j], lru_b_r[j],
                            lru_w_i[j], lru_b_i[j], lru_lambda[j], lru_w_out[j])
        x = x + g * y
        h, g = sublayer_input(x, norm_g[layer, 2], mod[:, 2])
        x = x + MACARON_W * g * swiglu(h, ffn_w_gu[layer, 1], ffn_w_down[layer, 1])
    return rmsnorm(x, final_norm_g)


DEPTH_2 = 4

CHUNK = 64
N_MIXERS_2 = 3

MLA_HEADS = 16
QK_NOPE = 64
QK_ROPE = 32
V_HEAD = 64
Q_LORA = 384
KV_LORA = 256
ROPE_THETA = 10000.0

CONV_WIDTH = 31

POOL_WINDOWS = (2, 4, 8, 16)
POOL_GROUPS = len(POOL_WINDOWS)

D_FF_2 = 4 * D_MODEL

NORM_EPS = 1e-6
NEG_INF = -1e30


def _rmsnorm(x, g):
    x32 = x.astype(jnp.float32)
    y = x32 * lax.rsqrt(jnp.mean(x32 * x32, axis=-1, keepdims=True) + NORM_EPS)
    return (y * g.astype(jnp.float32)).astype(x.dtype)

def _layernorm(x, g, b):
    x32 = x.astype(jnp.float32)
    mu = jnp.mean(x32, axis=-1, keepdims=True)
    xc = x32 - mu
    y = xc * lax.rsqrt(jnp.mean(xc * xc, axis=-1, keepdims=True) + NORM_EPS)
    return (y * g.astype(jnp.float32) + b.astype(jnp.float32)).astype(x.dtype)

def _rope_tables(positions):
    inv_freq = ROPE_THETA ** (-jnp.arange(0, QK_ROPE, 2, dtype=jnp.float32) / QK_ROPE)
    ang = positions.astype(jnp.float32)[..., None] * inv_freq
    return jnp.cos(ang), jnp.sin(ang)

def _apply_rope(x, cos, sin):
    half = x.shape[-1] // 2
    x1 = x[..., :half].astype(jnp.float32)
    x2 = x[..., half:].astype(jnp.float32)
    out = jnp.concatenate([x1 * cos - x2 * sin, x1 * sin + x2 * cos], axis=-1)
    return out.astype(x.dtype)

def _chunk_causal_attention(q, k, v):
    B, S, H, Dk = q.shape
    nb = S // Q_BLOCK
    qb = q.reshape(B, nb, Q_BLOCK, H, Dk).swapaxes(0, 1)
    k_chunk = jnp.arange(S) // CHUNK
    scale = 1.0 / math.sqrt(Dk)

    def one_block(args):
        qblk, bi = args
        q_chunk = (bi * Q_BLOCK + jnp.arange(Q_BLOCK)) // CHUNK
        mask = k_chunk[None, :] <= q_chunk[:, None]
        s = jnp.einsum('bqhd,bkhd->bhqk', qblk, k).astype(jnp.float32) * scale
        s = jnp.where(mask[None, None], s, NEG_INF)
        p = jax.nn.softmax(s, axis=-1).astype(v.dtype)
        return jnp.einsum('bhqk,bkhd->bqhd', p, v)

    o = lax.map(one_block, (qb, jnp.arange(nb)))
    return o.swapaxes(0, 1).reshape(B, S, H, v.shape[-1])

def _mla(h, positions, w_dq, q_norm_g, w_uq, w_dkv, kv_norm_g, w_ukv, w_o):
    B, S, _ = h.shape
    cq = _rmsnorm(h @ w_dq, q_norm_g)
    q = (cq @ w_uq).reshape(B, S, MLA_HEADS, QK_NOPE + QK_ROPE)
    q_nope, q_rope = q[..., :QK_NOPE], q[..., QK_NOPE:]
    ckv_all = h @ w_dkv
    ckv = _rmsnorm(ckv_all[..., :KV_LORA], kv_norm_g)
    k_rope = ckv_all[..., KV_LORA:]
    kv = (ckv @ w_ukv).reshape(B, S, MLA_HEADS, QK_NOPE + V_HEAD)
    k_nope, v = kv[..., :QK_NOPE], kv[..., QK_NOPE:]
    cos, sin = _rope_tables(positions)
    q_rope = _apply_rope(q_rope, cos[:, :, None], sin[:, :, None])
    k_rope = _apply_rope(k_rope, cos, sin)
    qf = jnp.concatenate([q_nope, q_rope], axis=-1)
    kf = jnp.concatenate(
        [k_nope, jnp.broadcast_to(k_rope[:, :, None], (B, S, MLA_HEADS, QK_ROPE))], axis=-1)
    o = _chunk_causal_attention(qf, kf, v)
    return o.reshape(B, S, MLA_HEADS * V_HEAD) @ w_o

def _conformer_conv(h, w_pw1, b_pw1, w_dw, b_dw, ln_g, ln_b, w_pw2, b_pw2):
    D = h.shape[-1]
    a = h @ w_pw1 + b_pw1
    u = a[..., :D] * jax.nn.sigmoid(a[..., D:])
    u = lax.conv_general_dilated(
        u, w_dw[:, None, :].astype(u.dtype), window_strides=(1,),
        padding=[(CONV_WIDTH - 1, 0)], dimension_numbers=('NWC', 'WIO', 'NWC'),
        feature_group_count=D) + b_dw
    u = jax.nn.silu(_layernorm(u, ln_g, ln_b))
    return u @ w_pw2 + b_pw2

def _pool_mixer(h, w, b, scale):
    B, S, D = h.shape
    C = D // POOL_GROUPS
    csum = jnp.cumsum(h.astype(jnp.float32), axis=1)
    t = jnp.arange(S)
    pooled = []
    for g, win in enumerate(POOL_WINDOWS):
        cs = csum[..., g * C:(g + 1) * C]
        lag = jnp.pad(cs, ((0, 0), (win, 0), (0, 0)))[:, :S]
        cnt = jnp.minimum(t + 1, win).astype(jnp.float32)
        pooled.append((cs - lag) / cnt[None, :, None])
    p = jnp.concatenate(pooled, axis=-1).astype(h.dtype) - h
    y = jnp.einsum('bsgc,gcd->bsgd', p.reshape(B, S, POOL_GROUPS, C), w) + b
    return y.reshape(B, S, D) * scale

def _sq_relu_mlp(h, w1, w2):
    return jnp.square(jax.nn.relu(h @ w1)) @ w2

def second_inputs(seed: int = 0) -> dict:
    key = jax.random.key(seed)
    ks = jax.random.split(key, 32)
    D = D_MODEL
    n_mla = (DEPTH_2 + 2) // 3
    n_conv = (DEPTH_2 + 1) // 3
    n_pool = DEPTH_2 // 3
    C = D // POOL_GROUPS

    def nrm(k, shape, fan_in, mult=1.0):
        return jax.random.normal(k, shape, jnp.float32) * (mult * fan_in ** -0.5)

    def gain(k, shape):
        return 1.0 + 0.05 * jax.random.normal(k, shape, jnp.float32)

    def bias(k, shape):
        return 0.02 * jax.random.normal(k, shape, jnp.float32)

    x = jax.random.normal(ks[0], (BATCH, SEQ, D), jnp.float32)
    c = jax.random.normal(ks[1], (BATCH, D), jnp.float32)
    offsets = jax.random.randint(ks[2], (BATCH,), 0, 64, dtype=jnp.int32) * CHUNK
    positions = offsets[:, None] + jnp.arange(SEQ, dtype=jnp.int32)[None, :]
    return {
        "x": x,
        "c": c,
        "positions": positions,
        "ada_w": nrm(ks[3], (DEPTH_2, D, 6 * D), D, 0.5),
        "ada_b": bias(ks[4], (DEPTH_2, 6 * D)),
        "norm_g": gain(ks[5], (DEPTH_2, 4, D)),
        "mla_w_dq": nrm(ks[6], (n_mla, D, Q_LORA), D),
        "mla_q_norm_g": gain(ks[7], (n_mla, Q_LORA)),
        "mla_w_uq": nrm(ks[8], (n_mla, Q_LORA, MLA_HEADS * (QK_NOPE + QK_ROPE)), Q_LORA),
        "mla_w_dkv": nrm(ks[9], (n_mla, D, KV_LORA + QK_ROPE), D),
        "mla_kv_norm_g": gain(ks[10], (n_mla, KV_LORA)),
        "mla_w_ukv": nrm(ks[11], (n_mla, KV_LORA, MLA_HEADS * (QK_NOPE + V_HEAD)), KV_LORA),
        "mla_w_o": nrm(ks[12], (n_mla, MLA_HEADS * V_HEAD, D), MLA_HEADS * V_HEAD),
        "conv_w_pw1": nrm(ks[13], (n_conv, D, 2 * D), D),
        "conv_b_pw1": bias(ks[14], (n_conv, 2 * D)),
        "conv_w_dw": nrm(ks[15], (n_conv, CONV_WIDTH, D), CONV_WIDTH),
        "conv_b_dw": bias(ks[16], (n_conv, D)),
        "conv_ln_g": gain(ks[17], (n_conv, D)),
        "conv_ln_b": bias(ks[18], (n_conv, D)),
        "conv_w_pw2": nrm(ks[19], (n_conv, D, D), D),
        "conv_b_pw2": bias(ks[20], (n_conv, D)),
        "pool_w": nrm(ks[21], (n_pool, POOL_GROUPS, C, C), C),
        "pool_b": bias(ks[22], (n_pool, POOL_GROUPS, C)),
        "pool_scale": gain(ks[23], (n_pool, D)),
        "ffn_w1": nrm(ks[24], (DEPTH_2, D, D_FF_2), D),
        "ffn_w2": nrm(ks[25], (DEPTH_2, D_FF_2, D), D_FF_2),
    }

def second_block(x, c, positions, ada_w, ada_b, norm_g,
              mla_w_dq, mla_q_norm_g, mla_w_uq, mla_w_dkv, mla_kv_norm_g, mla_w_ukv, mla_w_o,
              conv_w_pw1, conv_b_pw1, conv_w_dw, conv_b_dw, conv_ln_g, conv_ln_b,
              conv_w_pw2, conv_b_pw2,
              pool_w, pool_b, pool_scale,
              ffn_w1, ffn_w2):
    c_act = jax.nn.silu(c)
    for i in range(DEPTH_2):
        kind = i % N_MIXERS_2
        j = i // N_MIXERS_2
        mod = c_act @ ada_w[i] + ada_b[i]
        sh_m, sc_m, gt_m, sh_f, sc_f, gt_f = jnp.split(mod, 6, axis=-1)

        h = _rmsnorm(x, norm_g[i, 0]) * (1.0 + sc_m[:, None]) + sh_m[:, None]
        if kind == 0:
            y = _mla(h, positions, mla_w_dq[j], mla_q_norm_g[j], mla_w_uq[j],
                     mla_w_dkv[j], mla_kv_norm_g[j], mla_w_ukv[j], mla_w_o[j])
        elif kind == 1:
            y = _conformer_conv(h, conv_w_pw1[j], conv_b_pw1[j], conv_w_dw[j], conv_b_dw[j],
                                conv_ln_g[j], conv_ln_b[j], conv_w_pw2[j], conv_b_pw2[j])
        else:
            y = _pool_mixer(h, pool_w[j], pool_b[j], pool_scale[j])
        x = x + gt_m[:, None] * _rmsnorm(y, norm_g[i, 1])

        h = _rmsnorm(x, norm_g[i, 2]) * (1.0 + sc_f[:, None]) + sh_f[:, None]
        y = _sq_relu_mlp(h, ffn_w1[i], ffn_w2[i])
        x = x + gt_f[:, None] * _rmsnorm(y, norm_g[i, 3])
    return x


_first_inputs = second_inputs


def second_inputs(seed=0):
    import zlib

    import numpy as np

    out = dict(_first_inputs(seed))
    spreads = {}
    factors = {'mla_q_norm_g': 7.452,
     'conv_b_pw1': 8.0,
     'conv_b_dw': 5.391,
     'conv_ln_g': 3.486,
     'conv_ln_b': 8.0,
     'conv_b_pw2': 6.046,
     'pool_b': 3.132,
     'pool_scale': 4.653}
    for name, (base, spread) in spreads.items():
        noise = np.random.default_rng([zlib.crc32(name.encode()), seed]).standard_normal(out[name].shape)
        drawn = base * np.exp(spread * noise) if base else spread * noise
        out[name] = __import__('jax').numpy.asarray(drawn.astype(out[name].dtype))
    for name, factor in factors.items():
        out[name] = (out[name] * factor).astype(out[name].dtype)
    return out


_narrow_inputs = second_inputs


def second_inputs(seed=0):

    out = dict(_narrow_inputs(seed))
    wider = {'conv_ln_g': 3.63, 'conv_ln_b': 4.25, 'conv_b_pw2': 4.24, 'pool_scale': 4.02}
    for name, times in wider.items():
        mean = out[name].mean()
        out[name] = (mean + times * (out[name] - mean)).astype(out[name].dtype)
    return out


def setup_inputs(seed=0):
    out = dict(first_inputs(seed))
    for name, value in second_inputs(seed + 1).items():
        if name != "x":
            out[name + "_2"] = value
    return out


def reference(
    x, c, mod_w, mod_b, norm_g, ffn_w_gu, ffn_w_down, sb_w_qkv, sb_w_o, lru_w_in, lru_conv_w,
    lru_conv_b, lru_w_r, lru_b_r, lru_w_i, lru_b_i, lru_lambda, lru_w_out, final_norm_g, c_2,
    positions_2, ada_w_2, ada_b_2, norm_g_2, mla_w_dq_2, mla_q_norm_g_2, mla_w_uq_2,
    mla_w_dkv_2, mla_kv_norm_g_2, mla_w_ukv_2, mla_w_o_2, conv_w_pw1_2, conv_b_pw1_2,
    conv_w_dw_2, conv_b_dw_2, conv_ln_g_2, conv_ln_b_2, conv_w_pw2_2, conv_b_pw2_2, pool_w_2,
    pool_b_2, pool_scale_2, ffn_w1_2, ffn_w2_2,
):
    x = first_block(
        x, c, mod_w, mod_b, norm_g, ffn_w_gu, ffn_w_down, sb_w_qkv, sb_w_o, lru_w_in,
        lru_conv_w, lru_conv_b, lru_w_r, lru_b_r, lru_w_i, lru_b_i, lru_lambda, lru_w_out,
        final_norm_g,
    )
    return second_block(
        x, c_2, positions_2, ada_w_2, ada_b_2, norm_g_2, mla_w_dq_2, mla_q_norm_g_2, mla_w_uq_2,
        mla_w_dkv_2, mla_kv_norm_g_2, mla_w_ukv_2, mla_w_o_2, conv_w_pw1_2, conv_b_pw1_2,
        conv_w_dw_2, conv_b_dw_2, conv_ln_g_2, conv_ln_b_2, conv_w_pw2_2, conv_b_pw2_2,
        pool_w_2, pool_b_2, pool_scale_2, ffn_w1_2, ffn_w2_2,
    )


_drawn_inputs = setup_inputs


def setup_inputs(seed=0):
    import zlib

    import numpy as np

    out = dict(_drawn_inputs(seed))
    spreads = {}
    factors = {'lru_b_r': 4.537}
    for name, (base, spread) in spreads.items():
        noise = np.random.default_rng([zlib.crc32(name.encode()), seed]).standard_normal(out[name].shape)
        drawn = base * np.exp(spread * noise) if base else spread * noise
        out[name] = __import__('jax').numpy.asarray(drawn.astype(out[name].dtype))
    for name, factor in factors.items():
        out[name] = (out[name] * factor).astype(out[name].dtype)
    return out
```

```python
from contextlib import ExitStack

import numpy as np

import concourse.bass as bass
from concourse import mybir

F32 = mybir.dt.float32
F32R = mybir.dt.float32r
I32 = mybir.dt.int32
ALU = mybir.AluOpType
ACT = mybir.ActivationFunctionType
AX_X = mybir.AxisListType.X

P = 128
D = 1024
S = 256
KD = D // P
F1 = 2816
F2 = 4096
DR = 1280
NB = DR // P
HEADS, DH = 16, 64
NOPE, ROPE, VH = 64, 32, 64
QL, KVL = 384, 256
TAPS, WIDTH = 4, 31
EPS = 1e-6
NEG = -1e30
WINDOWS = (2, 4, 8, 16)
PADP = WINDOWS[-1]
THETA = 10000.0
MODC = 3 * D

CH = 2048
PC = CH // 2
RAWS = 4
OPS = 4
MODW = MODC // 2
ARENA = 2 * F2 // P * S
UNITS = KD * MODC // MODW


def param_rows(shapes):
    at, n = {}, 0
    for name, count in shapes:
        at[name] = n
        n += count
    return at, n


class Counts:

    def __init__(self):
        self.n = {}

    def get(self, what):
        return self.n.get(what, 0)

    def add(self, what, by):
        self.n[what] = self.get(what) + by

    def next(self, what):
        self.add(what, 1)
        return self.get(what) - 1


def two_pi_parts():
    a = 6.28125
    b = float((np.float32(2 * np.pi - a).view(np.uint32) & np.uint32(0xFFFFF000)).view(np.float32))
    return a, b, float(2 * np.pi - a - b)


def tiles(pair, width=2):
    return bass.ds(pair * width, width)


def as_rows(a):
    names = "abcd"[:len(a.shape) - 1]
    return a.rearrange(f"{' '.join(names)} (n p) -> ({' '.join(names)} n) p", p=P)


def build(nc, t, out, stop=None):
    ctx = ExitStack()

    def sb(name, shape, dt=F32):
        return ctx.enter_context(nc.sbuf_tensor(name, shape, dt))

    def sem(name):
        return ctx.enter_context(nc.semaphore(name))

    with ctx:
        raw = sb("raw", [P, RAWS, CH])
        w_hi = sb("w_hi", [P, OPS, PC], F32R)
        w_lo = sb("w_lo", [P, OPS, PC], F32R)
        mod_raw = sb("mod_raw", [P, 2, MODW])
        mod_acc = sb("mod_acc", [P, MODC])
        x = sb("x", [P, KD, S])
        tmp = sb("tmp", [P, KD, S])
        a_hi = sb("a_hi", [P, KD, S], F32R)
        a_lo = sb("a_lo", [P, KD, S], F32R)
        sig = sb("sig", [P, 2, 2, S])
        ev = sb("ev", [P, 2, 2, S])
        ones = sb("ones", [P, P])
        one1 = sb("one1", [P, P])
        tri = sb("tri", [P, P])
        ident = sb("ident", [P, P])
        eps_col = sb("eps_col", [P, 1])
        lsp = sb("lsp", [P, 6, NB])
        rms = sb("rms", [P, 2, S])
        inv = sb("inv", [P, 2, S])
        rope = sb("rope", [P, S])
        rcol = sb("rcol", [P, 2])
        share = sb("share", [P, len(WINDOWS), PADP])
        top = sb("top", [P, HEADS, 2])
        low = sb("low", [P, HEADS, 2])
        total = sb("total", [P, HEADS, 2])
        part = sb("part", [P, HEADS, 2])
        cact = sb("cact", [P, 2 * KD])
        mv = sb("mv", [P, 14, 24])
        mv_a = sb("mv_a", [P, 14, KD])
        mv_g = sb("mv_g", [P, 14, KD])

        vec = [("mod_b", 2 * 72), ("norm_g", 48), ("final_norm_g", 8), ("c", 8),
               ("lru_conv_w", 40), ("lru_conv_b", 10), ("lru_b_r", 10), ("lru_b_i", 10), ("lru_lambda", 10),
               ("c_2", 8), ("ada_b_2", 4 * 48), ("norm_g_2", 4 * 4 * 8), ("mla_q_norm_g_2", 6),
               ("mla_kv_norm_g_2", 4), ("conv_b_pw1_2", 16), ("conv_w_dw_2", 8 * WIDTH), ("conv_b_dw_2", 8),
               ("conv_ln_g_2", 8), ("conv_ln_b_2", 8), ("conv_b_pw2_2", 8), ("pool_b_2", 8),
               ("pool_scale_2", 8)]
        ROW, NROW = param_rows(vec)
        vectors = {name: as_rows(t[name]) for name, _ in vec}
        for name, count in vec:
            assert vectors[name].shape[0] == count, (name, vectors[name].shape, count)
        NLOADS = 1 + sum((ROW[n] + m - 1) // P - ROW[n] // P + 1 for n, m in vec)
        NPT = -(-NROW // P)
        assert NPT <= 8
        cols = sb("cols", [P, NPT * P])

        def col(name, i, n=1):
            return cols[:, ROW[name] + i:ROW[name] + i + n]

        base = nc.sbuf_base
        arena = sb("arena", [P, ARENA])

        def place(layout):
            at, got = base, {}
            for name, shape, dt in layout:
                got[name] = nc.alloc_sbuf_tensor_at(name, shape, dt, offset=at)
                at += -(-4 * int(np.prod(shape[1:])) // 32) * 32
            assert at <= base + 4 * ARENA, (layout[0][0], at - base)
            return got

        v = place([("hid_hi", [P, 32, S], F32R), ("hid_lo", [P, 32, S], F32R)])
        hid_hi, hid_lo = v["hid_hi"], v["hid_lo"]
        v = place([("rows", [P, NPT, P], F32), ("xin", [P, 2, D], F32), ("rrow", [1, 2, P], F32),
                   ("pos_i", [1, S], I32), ("pos_f", [1, S], F32), ("turns_i", [P, S], I32)])
        rows, xin, rrow, pos_i, pos_f, turns_i = (v[n] for n in ("rows", "xin", "rrow", "pos_i", "pos_f", "turns_i"))
        v = place([("qk", [P, 2 * KD, S], F32), ("vt", [P, 2, D], F32), ("sb_z", [P, 4, 384], F32),
                   ("sb_n", [P, 4, 384], F32), ("sb_l", [P, 4, 384], F32), ("sb_s", [P, 4, 384], F32),
                   ("sb_w", [P, 4, 384], F32)])
        qk, vt, sb_z, sb_n, sb_l, sb_s, sb_w = (v[n] for n in ("qk", "vt", "sb_z", "sb_n", "sb_l", "sb_s", "sb_w"))
        XP = S + TAPS - 1
        v = place([("lw", [P, 2 * NB, P], F32), ("lg", [P, NB, S], F32), ("lxb", [P, NB, XP], F32),
                   ("lxc", [P, NB, S], F32), ("lri", [P, NB, 2, S], F32)])
        lg, lxb, lxc, lw, lri = (v[n] for n in ("lg", "lxb", "lxc", "lw", "lri"))
        v = place([("more_hi", [P, NB - KD, S], F32R), ("more_lo", [P, NB - KD, S], F32R)])
        more_hi, more_lo = v["more_hi"], v["more_lo"]

        def y_hi(n):
            return a_hi[:, n, :] if n < KD else more_hi[:, n - KD, :]

        def y_lo(n):
            return a_lo[:, n, :] if n < KD else more_lo[:, n - KD, :]
        UP = S + WIDTH - 1
        CONV_DVE = 5
        v = place([("cu", [P, KD, UP], F32), ("cacc", [P, KD, S], F32), ("diag", [P, KD - CONV_DVE, WIDTH, P], F32)])
        cu, cacc, diag = v["cu"], v["cacc"], v["diag"]
        PP = S + PADP
        v = place([("ph", [P, KD, PP], F32), ("pa", [P, KD, PP], F32), ("pb", [P, KD, PP], F32), ("pp", [P, KD, S], F32)])
        ph, pa, pb, pp = (v[n] for n in ("ph", "pa", "pb", "pp"))
        v = place([("qf", [P, HEADS, S], F32), ("kf", [P, HEADS, S], F32), ("mvt", [P, 2, D], F32),
                   ("cn", [P, 5, S], F32), ("cn_hi", [P, 5, S], F32R), ("cn_lo", [P, 5, S], F32R),
                   ("seen", [P, 384], F32), ("mp", [P, 4, 384], F32)])
        qf, kf, mvt, cn, cn_hi, cn_lo, seen, mp = (
            v[n] for n in ("qf", "kf", "mvt", "cn", "cn_hi", "cn_lo", "seen", "mp"))
        mpt = tmp[:, 0:6, :].rearrange("p k s -> p (k s)").rearrange("p (n q) -> p n q", q=384)
        oout = place([("oout", [P, 2, D], F32)])["oout"]
        bk = ctx.enter_context(nc.psum_tensor("bk", [P, 8, 512], F32))

        landed = [sem(f"landed{i}") for i in range(RAWS)]
        hi_ready = sem("hi_ready")
        lo_ready = sem("lo_ready")
        piece_used = sem("piece_used")
        bank_free = [sem("bank_free0"), sem("bank_free1")]
        mod_landed = [sem(f"mod_landed{i}") for i in range(2)]
        mod_used = sem("mod_used")
        turn_done = sem("turn_done")
        turn_read = sem("turn_read")
        mod_ready = sem("mod_ready")
        sq_ready = sem("sq_ready")
        mean_done = sem("mean_done")
        rms_ready = sem("rms_ready")
        xn_ready = sem("xn_ready")
        h_ready = sem("h_ready")
        ahi_ready = sem("ahi_ready")
        act_ready = sem("act_ready")
        sig_ready = sem("sig_ready")
        hhi_ready = sem("hhi_ready")
        hid_ready = sem("hid_ready")
        z_done = sem("z_done")
        z_copied = sem("z_copied")
        n_ready = sem("n_ready")
        e1_ready = sem("e1_ready")
        l_ready = sem("l_ready")
        sp_ready = sem("sp_ready")
        spm_ready = sem("spm_ready")
        suf_done = sem("suf_done")
        t_ready = sem("t_ready")
        e_ready = sem("e_ready")
        w_ready = sem("w_ready")
        o_done = sem("o_done")
        ohi_ready = sem("ohi_ready")
        oact_ready = sem("oact_ready")
        lw_landed = sem("lw_landed")
        xb_zero = sem("xb_zero")
        xc_first = sem("xc_first")
        xc_ready = sem("xc_ready")
        ri_done = sem("ri_done")
        ri_ready = sem("ri_ready")
        ix_ready = sem("ix_ready")
        a_ready = sem("a_ready")
        v_ready = sem("v_ready")
        s_ready = sem("s_ready")
        y_ready = sem("y_ready")
        lact_ready = sem("lact_ready")
        x_done = sem("x_done")
        prod_ready = sem("prod_ready")
        pos_landed = sem("pos_landed")
        pool_landed = sem("pool_landed")
        pos_ready = sem("pos_ready")
        rope_read = sem("rope_read")
        rope_in = sem("rope_in")
        rope_arg = sem("rope_arg")
        rope_ready = sem("rope_ready")
        kv_done = sem("kv_done")
        ckv_out = sem("ckv_out")
        nope_out = sem("nope_out")
        cnh_ready = sem("cnh_ready")
        cn_ready = sem("cn_ready")
        qf_ready = sem("qf_ready")
        kr_ready = sem("kr_ready")
        seen_ready = sem("seen_ready")
        s_done = sem("s_done")
        sm_ready = sem("sm_ready")
        low_ready = sem("low_ready")
        p_ready = sem("p_ready")
        part_ready = sem("part_ready")
        pn_ready = sem("pn_ready")
        pt_done = sem("pt_done")
        pt_ready = sem("pt_ready")
        pool_done = sem("pool_done")
        cu_zero = sem("cu_zero")
        csig_ready = sem("csig_ready")
        conv_dve = sem("conv_dve")
        diag_ready = sem("diag_ready")
        dw_done = sem("dw_done")
        conv_act = sem("conv_act")
        xc2_ready = sem("xc2_ready")
        ph_zero = sem("ph_zero")
        pp_ready = sem("pp_ready")
        consts = sem("consts")
        loaded = sem("loaded")
        cact_ready = sem("cact_ready")
        dve_step = sem("dve_step")
        pool_step = sem("pool_step")
        out_ready = sem("out_ready")
        stored = sem("stored")

        kinds = ["ffn1", "sb", "ffn1", "ffn1", "lru", "ffn1", "mla", "ffn2", "conv", "ffn2", "pool", "ffn2", "mla", "ffn2"]
        CHUNKS = {"ffn1": 34, "sb": 16, "lru": 16, "mla": 14, "ffn2": 32, "conv": 12, "pool": 1}
        WJOBS = {"ffn1": 13, "sb": 8, "lru": 7, "mla": 12, "ffn2": 10, "conv": 7, "pool": 2}
        PAIRS = {"ffn1": 11, "ffn2": 16}
        stages, c, w, hid, grp = [], 0, 0, 0, 1
        for n, kind in enumerate(kinds):
            groups = [g for g in (grp, grp + 1) if g < len(kinds)] if kind in PAIRS else []
            late = stages[-1]["groups"][1] if n and len(stages[-1]["groups"]) > 1 else None
            stages.append(dict(kind=kind, late=late, n=n, c=c, w=w, hid=hid, groups=groups, nth=kinds[:n].count(kind)))
            c, w, hid, grp = c + CHUNKS[kind], w + WJOBS[kind], hid + PAIRS.get(kind, 0), grp + len(groups)
        if stop is not None:
            stages = stages[:stop]
        LAST_GROUP = max([0] + [h for z in stages for h in z["groups"]])
        st_pool = [z for z in stages if z["kind"] == "pool"]
        NPIECE = 2 * (stages[-1]["c"] + CHUNKS[stages[-1]["kind"]])
        act_base = [4 * (z["n"] + sum(y["kind"] == "conv" for y in stages[:z["n"]])) for z in stages]
        double = set()
        for st in stages:
            if st["kind"] == "ffn1":
                double |= {2 * (st["c"] + 27), 2 * (st["c"] + 33)}
            if st["kind"] == "lru":
                double |= {2 * (st["c"] + 12), 2 * (st["c"] + 15)}

        def split(p):
            h = p % 2
            whole = [(lambda o: o, lambda r: r[:, h * PC:h * PC + PC])]
            st = [z for z in stages if 2 * z["c"] <= p][-1]
            c = p // 2 - st["c"]
            if st["kind"] != "mla" or c >= 10:
                return whole
            if c >= 8:
                return [(lambda o, e=e: o[:, 512 * e:512 * e + 512].rearrange("p (h x) -> p h x", x=NOPE),
                         lambda r, e=e: r[:, h * PC:h * PC + PC].rearrange("p (h x) -> p h x", x=NOPE + VH)
                         [:, :, NOPE * e:NOPE * e + NOPE]) for e in range(2)]
            if c < 2:
                return [(lambda o: o[:, 0:2 * QL], lambda r: r[:, h * 2 * QL:(h + 1) * 2 * QL])]
            if c < 4:
                n, wide, at, cw = 2, KVL + ROPE, h * 2 * (KVL + ROPE), KVL + 2 * ROPE
                e = KVL
            else:
                n, wide, at, cw = (2 - h) * 4, NOPE + ROPE, h * 8 * (NOPE + ROPE), P
                e = NOPE
            o3 = lambda o: o[:, 0:n * cw].rearrange("p (a b) -> p a b", b=cw)
            r3 = lambda r: r[:, at:at + n * wide].rearrange("p (a b) -> p a b", b=wide)
            f = ROPE // 2
            return [(lambda o: o3(o)[:, :, 0:wide], lambda r: r3(r)),
                    (lambda o: o3(o)[:, :, wide:wide + f], lambda r: r3(r)[:, :, e + f:e + ROPE]),
                    (lambda o: o3(o)[:, :, wide + f:wide + ROPE], lambda r: r3(r)[:, :, e:e + f])]

        def sq_pair(q):
            return (sig, ev)[q // 2][:, q % 2, :, :]

        MEAN_CONV = sum({"mla": 4}.get(z["kind"], 1 + (z["n"] >= 6)) for z in stages[:8]) + 3
        W_END = w if stop is None else stages[-1]["w"] + WJOBS[stages[-1]["kind"]]

        def lru_t(n):
            return tmp[:, n, :] if n < KD else sig[:, 0, n - KD, :]

        def mod_of(g):
            return (t["mod_w"][g // 3], g % 3 * MODC) if g < 6 else (t["ada_w_2"][(g - 6) // 2], (g - 6) % 2 * MODC)

        def mod_bias(g):
            return col("mod_b", 24 * g, 24) if g < 6 else col("ada_b_2", 24 * (g - 6), 24)

        def is_free(eng, w, i=0):
            eng.wait_ge(bank_free[w % 2], w // 2 + 1 + i)

        def is_read(eng, w, i=0):
            eng.wait_ge(bank_free[w % 2], w // 2 + 2 + i)

        def is_done(eng, c, i=0):
            eng.wait_ge(piece_used, OPS + 2 * c + 8 * i)

        def job_banks(w, n=4, width=S):
            return bk[:, 4 * (w % 2):4 * (w % 2) + n, 0:width]

        def job_flat(w, n):
            return bk[:, 4 * (w % 2):4 * (w % 2) + 4, :].rearrange("p b n -> p (b n)")[:, 0:n]

        block = ctx.enter_context(nc.Block())

        @block.sync
        def _(sp):
            def chunk(c, src, view, i=0):
                sp.wait_ge(lo_ready, 2 * c + 2 + 8 * i)
                sp.dma_start(view(raw[:, c % RAWS, :]), src).then_inc(landed[c % RAWS], 16)

            def plain(c, w, kt, n, col0, i=0):
                chunk(c, w[kt * P:(kt + n) * P, :][:, bass.ds(col0, 512)].rearrange("(k p) m -> p k m", p=P),
                      lambda r: r[:, 0:n * 512].rearrange("p (k m) -> p k m", m=512), i)

            def some(c, w, kt, n, col0, wide):
                chunk(c, w[kt * P:(kt + n) * P, col0:col0 + wide].rearrange("(k p) m -> p k m", p=P),
                      lambda r: r[:, 0:n * wide].rearrange("p (k m) -> p k m", m=wide))

            def narrow(c, w, col0, i=0):
                chunk(c, w[:, bass.ds(col0, 256)].rearrange("(k p) m -> p k m", p=P),
                      lambda r: r.rearrange("p (k m) -> p k m", m=256), i)

            sp.dma_start(pos_i[:, :], t["positions_2"]).then_inc(pos_landed, 16)
            sp.dma_start(xin[:, :, :], t["x"][0].rearrange("(b p) d -> p b d", p=P)).then_inc(loaded, 16)
            for name, count in vec:
                src, r = vectors[name], 0
                while r < count:
                    a = ROW[name] + r
                    n = min(count - r, P - a % P)
                    sp.dma_start(rows[a % P:a % P + n, a // P, :], src[r:r + n, :]).then_inc(loaded, 16)
                    r += n

            for st in stages:
                c = st["c"]
                if st["kind"] == "ffn1":
                    wg, wd = t["ffn_w_gu"][st["n"] // 3, st["n"] % 3 // 2], t["ffn_w_down"][st["n"] // 3, st["n"] % 3 // 2]
                    with sp.Fori(0, 5) as i:
                        for b in range(4):
                            narrow(c + b, wg, (2 * i + b // 2) * 256 + b % 2 * F1, i)
                    for b in range(2):
                        narrow(c + 20 + b, wg, 10 * 256 + b * F1)
                    for m in range(2):
                        for k in range(6):
                            plain(c + 22 + 6 * m + k, wd, 4 * k, min(4, 22 - 4 * k), 512 * m)
                elif st["kind"] == "sb":
                    with sp.Fori(0, 3) as i:
                        for b in range(4):
                            plain(c + b, t["sb_w_qkv"][0], 4 * (b % 2), 4, (2 * i + b // 2) * 512, i)
                    for b in range(4):
                        plain(c + 12 + b, t["sb_w_o"][0], 4 * (b % 2), 4, 512 * (b // 2))
                elif st["kind"] == "lru":
                    is_done(sp, c)
                    for g, name in enumerate(("lru_w_r", "lru_w_i")):
                        sp.dma_start(lw[:, g * NB:(g + 1) * NB, :], t[name][0].rearrange("n k j -> k n j"))\
                          .then_inc(lw_landed, 16)
                    with sp.Fori(0, 2) as i:
                        for b in range(4):
                            plain(c + b, t["lru_w_in"][0], 4 * (b % 2), 4, (2 * i + b // 2) * 512, i)
                    for b in range(2):
                        plain(c + 8 + b, t["lru_w_in"][0], 4 * b, 4, 2048)
                    for m in range(2):
                        for k in range(3):
                            plain(c + 10 + 3 * m + k, t["lru_w_out"][0], 4 * k, min(4, 10 - 4 * k), 512 * m)
                elif st["kind"] == "ffn2":
                    w1, w2 = t["ffn_w1_2"][st["nth"]], t["ffn_w2_2"][st["nth"]]
                    with sp.Fori(0, 4) as i:
                        for b in range(4):
                            narrow(c + b, w1, (4 * i + b) * 256, i)
                    for m in range(2):
                        for k in range(8):
                            plain(c + 16 + 8 * m + k, w2, 4 * k, 4, 512 * m)
                elif st["kind"] == "mla":
                    n = st["nth"]
                    for b in range(2):
                        some(c + b, t["mla_w_dq_2"][n], 4 * b, 4, 0, QL)
                    for b in range(2):
                        some(c + 2 + b, t["mla_w_dkv_2"][n], 4 * b, 4, 0, KVL + ROPE)
                    for b in range(4):
                        some(c + 4 + b, t["mla_w_uq_2"][n], 0, QL // P, b * 384, 384)
                    for b in range(2):
                        some(c + 8 + b, t["mla_w_ukv_2"][n], 0, KVL // P, b * 1024, 1024)
                    for b in range(4):
                        plain(c + 10 + b, t["mla_w_o_2"][n], 4 * (b % 2), 4, 512 * (b // 2))
                elif st["kind"] == "conv":
                    for b in range(8):
                        narrow(c + b, t["conv_w_pw1_2"][0], b // 2 * 256 + (1 - b % 2) * D)
                    for b in range(4):
                        plain(c + 8 + b, t["conv_w_pw2_2"][0], 4 * (b % 2), 4, 512 * (b // 2))
                elif st["kind"] == "pool":
                    sp.wait_ge(lo_ready, 2 * c + 2)
                    for kt in range(2):
                        sp.dma_start(raw[:, c % RAWS, kt * PC:(kt + 1) * PC].rearrange("p (g m) -> p g m", m=256),
                                     t["pool_w_2"][0].rearrange("g (k p) m -> k p g m", p=P)[kt])\
                            .then_inc(landed[c % RAWS] if kt else pool_landed, 16)
            sp.wait_ge(out_ready, 1)
            sp.dma_start(out[0].rearrange("(b p) d -> p b d", p=P), oout[:, :, :]).then_inc(stored, 16)
            sp.wait_ge(stored, 16)

        @block.gpsimd
        def _(pool):
            k = Counts()

            def mod_load(g, i, units):
                w, at = mod_of(g)
                for u in units:
                    pool.wait_ge(mod_used, UNITS * g + 4 * i + u + 1)
                    pool.dma_start(mod_raw[:, u % 2, :].unsqueeze(1),
                                   w.rearrange("(k p) m -> p k m", p=P)[:, bass.ds(2 * i + u // 2, 1),
                                       at + u % 2 * MODW:at + (u % 2 + 1) * MODW]).then_inc(mod_landed[u % 2], 16)

            def mod_next(g, u):
                if u < UNITS:
                    mod_load(g, u // 4, range(u % 4, u % 4 + 2))
                elif g < LAST_GROUP:
                    mod_load(g + 1, 0, range(2))

            def mod_stream(g, beside=None):
                with pool.Fori(0, 3) as i:
                    for b in range(2):
                        mod_load(g, i, range(2 * b + 2, 2 * b + 4))
                        if beside is not None:
                            beside(i, b)
                for b in range(2):
                    mod_next(g, 14 + 2 * b)
                    if beside is not None:
                        beside(3, b)

            def act_low():
                for q in range(4):
                    pool.wait_ge(ahi_ready, k.next("ahi") + 1)
                    pool.tensor_tensor(a_lo[:, 2 * q:2 * q + 2, :], tmp[:, 2 * q:2 * q + 2, :],
                                       a_hi[:, 2 * q:2 * q + 2, :].bitcast(F32), ALU.subtract).then_inc(act_ready, 1)

            def hid_low(n, pair, slot, width=2):
                pool.wait_ge(hhi_ready, n + 1)
                pool.tensor_tensor(hid_lo[:, tiles(pair, width), :], ev[:, slot, :, :],
                                   hid_hi[:, tiles(pair, width), :].bitcast(F32), ALU.subtract).then_inc(hid_ready, 1)

            def keep_earlier(buf, ready, n, done):
                diag = buf.rearrange("p (b q) -> p b q", q=P)[:, 0:3:2, :]
                pool.wait_ge(ready, n)
                pool.affine_select(out=diag, in_=diag, compare_op=ALU.is_gt, fill=0.0, base=0,
                                   pattern=[[0, 2], [1, P]], channel_multiplier=-1).then_inc(done, 1)

            pool.memset(eps_col[:, :], EPS)
            for g, win in enumerate(WINDOWS):
                pool.memset(share[:, g, :], 1.0 / win)
            freqs = np.power(np.float32(THETA), -np.arange(0, ROPE, 2, dtype=np.float32) / np.float32(ROPE))
            pool.memset(rrow[:, 0, 0:NOPE], 0.0)
            for f in range(ROPE // 2):
                pool.memset(rrow[:, 0, NOPE + f:P:ROPE // 2], float(freqs[f]))
            pool.memset(rrow[:, 1, :], 1.0).then_inc(pool_step, 1)
            pool.wait_ge(pool_step, 1)
            pool.memset(rrow[:, 1, 96:112], -1.0)
            for g, win in enumerate(WINDOWS):
                for s in range(win):
                    pool.memset(share[:, g, s:s + 1], 1.0 / (s + 1))
            pool.memset(ones[:, :], 1.0 / D).then_inc(consts, 1)
            pool.memset(one1[:, :], 1.0).then_inc(consts, 1)
            pool.memset(ident[:, :], 0.0).then_inc(pool_step, 1)
            pool.wait_ge(pool_step, 2)
            pool.affine_select(out=ident[:, :], in_=ident[:, :], compare_op=ALU.not_equal, fill=1.0, base=0,
                               pattern=[[-1, P]], channel_multiplier=1).then_inc(consts, 1)
            pool.wait_ge(consts, 2)
            pool.affine_select(out=tri[:, :], in_=one1[:, :], compare_op=ALU.is_ge, fill=0.0, base=0,
                               pattern=[[-1, P]], channel_multiplier=1).then_inc(consts, 1)
            mod_load(0, 0, range(2))
            mod_stream(0)

            def heads_low():
                for n in range(HEADS):
                    pool.wait_ge(part_ready, k.next("part") + 1)
                    for a in range(2):
                        b = mp[:, n % 4, P * a:P + 2 * P * a]
                        ins = pool.tensor_scalar(b, b, part[:, n, a:a + 1], None, ALU.mult)
                    ins.then_inc(pn_ready, 1)

            for st in stages:
                if st["kind"] != "pool":
                    act_low()
                if st["kind"] == "ffn2":
                    g, n = st["groups"], st["hid"]

                    def two_low(i, b):
                        for e in range(2):
                            hid_low(n + 4 * i + 2 * b + e, 4 * i + 2 * b + e, e)

                    if g:
                        mod_stream(g[0], two_low)
                    else:
                        with pool.Fori(0, 4) as i:
                            for b in range(2):
                                two_low(i, b)
                    if len(g) > 1:
                        mod_stream(g[1])
                elif st["kind"] == "mla":
                    pool.memset(seen[:, :], 0.0).then_inc(pool_step, 1)
                    pool.wait_ge(pool_step, 3 + k.next("pstep"))
                    pool.memset(seen[0:64, 64:P], NEG)
                    pool.memset(seen[0:64, 320:384], NEG).then_inc(seen_ready, 1)
                    for a, b in ((0, 2), (2, 3), (3, 5)):
                        pool.wait_ge(cnh_ready, k.next("cn") + 1)
                        pool.tensor_tensor(cn_lo[:, a:b, :], cn[:, a:b, :], cn_hi[:, a:b, :].bitcast(F32), ALU.subtract)\
                            .then_inc(cn_ready, 1)
                    heads_low()
                elif st["kind"] == "conv":
                    pool.memset(cu[:, :, 0:WIDTH - 1], 0.0).then_inc(cu_zero, 1)
                    for n in range(CONV_DVE, KD):
                        for tap in range(WIDTH):
                            ins = pool.tensor_scalar(diag[:, n - CONV_DVE, tap, :], ident[:, :],
                                                     col("conv_w_dw_2", KD * tap + n), None, ALU.mult)
                        ins.then_inc(diag_ready, 1)
                    act_low()
                elif st["kind"] == "pool":
                    for buf in (ph, pa, pb):
                        ins = pool.memset(buf[:, :, 0:PADP], 0.0)
                    ins.then_inc(ph_zero, 1)
                    for q in range(4):
                        pool.wait_ge(pp_ready, q + 1)
                        pool.tensor_tensor(a_lo[:, 2 * q:2 * q + 2, :], pp[:, 2 * q:2 * q + 2, :],
                                           a_hi[:, 2 * q:2 * q + 2, :].bitcast(F32), ALU.subtract).then_inc(act_ready, 1)
                elif st["kind"] == "ffn1":
                    g, n = st["groups"][0], st["hid"]
                    mod_stream(g, lambda i, b: hid_low(n + 2 * i + b, 2 * i + b, b))
                    for b in range(3):
                        hid_low(n + 8 + b, 8 + b, b % 2)
                    mod_stream(g + 1)
                elif st["kind"] == "sb":
                    for n in range(HEADS + 2):
                        if n < HEADS:
                            keep_earlier(sb_s[:, n % 4, :], sp_ready, n + 1, spm_ready)
                        if n >= 2:
                            keep_earlier(sb_w[:, (n - 2) % 4, :], e_ready, n - 1, w_ready)
                elif st["kind"] == "lru":
                    pool.memset(lxb[:, :, 0:TAPS - 1], 0.0).then_inc(xb_zero, 1)
                    for n in range(NB):
                        pool.wait_ge(ri_ready, n + 1)
                        pool.tensor_tensor(lri[:, n, 1, :], lri[:, n, 1, :], lxc[:, n, :], ALU.mult)\
                            .then_inc(ix_ready, 1)
                    for n in range(NB):
                        pool.wait_ge(y_ready, n + 1)
                        pool.tensor_tensor(y_lo(n), lg[:, n, :], y_hi(n).bitcast(F32),
                                           ALU.subtract).then_inc(lact_ready, 1)

        @block.scalar
        def _(act):
            k = Counts()
            act.sem_inc(bank_free[0], 1)
            act.sem_inc(bank_free[1], 1)

            def pieces(a, b, i=0):
                for p in range(a, b):
                    c = p // 2
                    if p >= NPIECE or p - 1 in double:
                        continue
                    act.wait_ge(piece_used, p + 1 + 8 * i)
                    act.wait_ge(landed[c % RAWS], 16 * (c // RAWS + 1) + 16 * i)
                    if st_pool and p == 2 * st_pool[0]["c"]:
                        act.wait_ge(pool_landed, 16)
                    for o, r in split(p):
                        ins = act.activation(o(w_hi[:, p % OPS, :]), r(raw[:, c % RAWS, :]), ACT.Copy)
                    ins.then_inc(hi_ready, 2 if p in double else 1)

            def squares(src, dst, n):
                for q in range(0, n, 2):
                    act.activation(dst[:, q:min(q + 2, n), :], src[:, q:min(q + 2, n), :], ACT.Square)\
                        .then_inc(sq_ready, 1)

            def x_squares(w):
                for m in range(2):
                    if k.get("normed") == 0 and w:
                        is_read(act, w - 2 + m)
                    for q in range(2 * m, 2 * m + 2):
                        if k.get("normed"):
                            act.wait_ge(x_done, k.next("xd") + 1)
                        squares(x[:, 2 * q:2 * q + 2, :], tmp[:, 2 * q:2 * q + 2, :], 2)

            def root(w, scale=1.0):
                act.wait_ge(mean_done, k.next("mean") + 1)
                act.activation(rms[:, k.next("root") % 2, :], job_flat(w, S), ACT.Sqrt, bias=eps_col[:, 0:1], scale=scale).then_inc(rms_ready, 1)

            def modulate(func, scale, bias, out=None):
                for q in range(4):
                    act.wait_ge(xn_ready, k.next("xn") + 1)
                    for j in range(2 * q, 2 * q + 2):
                        ins = act.activation((out or (lambda j: tmp[:, j, :]))(j), tmp[:, j, :], func,
                                             bias=bias(j), scale=scale(j))
                    ins.then_inc(h_ready, 1)

            def final_norm(w):
                x_squares(w)
                root(w)
                k.add("normed", 1)

            def post_squares(w):
                for m in range(2):
                    is_read(act, w + m)
                    for q in range(2 * m, 2 * m + 2):
                        squares(tmp[:, 2 * q:2 * q + 2, :], sq_pair(q), 2)

            def y_out(w, m, bias=None):
                y = tmp[:, 4 * m:4 * m + 4, :]
                if bias is None:
                    act.activation(y, job_banks(w + m), ACT.Copy).then_inc(bank_free[(w + m) % 2], 1)
                    return
                for j in range(4):
                    ins = act.activation(y[:, j, :], job_banks(w + m)[:, j, :], ACT.Identity, bias=col(bias, 4 * m + j))
                ins.then_inc(bank_free[(w + m) % 2], 1)

            def heads_out(n):
                if n >= 0 and n % 2 == 0 and n // 2 < HEADS // 2:
                    act.wait_ge(o_done, k.next("o") + 1)
                    act.activation(a_hi[:, n // 2, :], bk[:, 4 + n // 2 % 2, 0:S], ACT.Copy).then_inc(ohi_ready, 1)

            act.wait_ge(consts, 1)
            act.wait_ge(turn_read, 2)
            act.activation(cact[:, 0:KD], col("c", 0, KD), ACT.Silu)
            act.activation(cact[:, KD:2 * KD], col("c_2", 0, KD), ACT.Silu)
            act.activation(lsp[:, 0, :], col("lru_lambda", 0, NB), ACT.Abs).then_inc(cact_ready, 1)
            act.wait_ge(cact_ready, 1)
            act.activation(lsp[:, 1, :], lsp[:, 0, :], ACT.Exp, scale=-1.0).then_inc(cact_ready, 1)
            act.wait_ge(rope_arg, 1)
            act.activation(rope[NOPE:P, :], ev[NOPE:P, 0, 0, :], ACT.Sin).then_inc(rope_ready, 1)
            pieces(0, 4)

            for st in stages:
                p, c, w, g = 2 * st["c"], st["c"], st["w"], st["n"]
                if g == 6:
                    final_norm(w)
                x_squares(w)
                root(w)
                act.wait_ge(mod_ready, g + 1)
                if st["kind"] == "pool":
                    act.wait_ge(ph_zero, 1)
                modulate(ACT.Identity, lambda j: mv_a[:, g, j:j + 1], lambda j: mv[:, g, j:j + 1],
                         (lambda j: ph[:, j, PADP:]) if st["kind"] == "pool" else None)
                if st["kind"] == "ffn2":
                    def relu(w, c, i, e):
                        is_done(act, c + 1 + e, i)
                        act.activation(sig[:, e, :, :], job_banks(w)[:, 2 * e:2 * e + 2, :], ACT.Relu).then_inc(sig_ready, 1)

                    with act.Fori(0, 4) as i:
                        for b in range(2):
                            pieces(p + 4 + 4 * b, p + 8 + 4 * b, i)
                            for e in range(2):
                                relu(w + b, c + 2 * b, i, e)
                            for e in range(2):
                                if e:
                                    is_read(act, w + b, i)
                                else:
                                    act.wait_ge(prod_ready, 8 * st["nth"] + 2 * i + b + 1)
                                act.activation(hid_hi[:, tiles(4 * i + 2 * b + e), :], ev[:, e, :, :], ACT.Copy)\
                                    .then_inc(hhi_ready, 1)
                    for m in range(2):
                        pieces(p + 36 + 16 * m, p + 52 + 16 * m)
                        is_done(act, c + 24 + 8 * m)
                        y_out(w + 8, m)
                    post_squares(w + 8)
                    root(w + 10)
                elif st["kind"] == "mla":
                    pieces(p + 4, p + 8)
                    is_done(act, c + 2)
                    act.activation(cn[:, 0:3, :], job_banks(w, 3), ACT.Copy).then_inc(bank_free[w % 2], 1)
                    is_read(act, w)
                    squares(cn[:, 0:2, :], sq_pair(0), 2)
                    squares(cn[:, 2:3, :], sq_pair(1)[:, 0:1, :], 1)
                    pieces(p + 8, p + 12)
                    is_done(act, c + 4)
                    act.activation(cn[:, 3:5, :], job_banks(w + 1, 2), ACT.Copy).then_inc(ckv_out, 1)
                    act.wait_ge(ckv_out, st["nth"] + 1)
                    squares(cn[:, 3:5, :], sq_pair(2), 2)
                    root(w + 2, D / QL)
                    root(w + 3, D / KVL)
                    for b in range(4):
                        pieces(p + 12 + 2 * b, p + 14 + 2 * b)
                        is_done(act, c + 5 + b)
                        act.activation(qf[0:NOPE, 4 * b:4 * b + 4, :], job_banks(w + 2 + b)[0:NOPE], ACT.Copy)\
                            .then_inc(nope_out, 1)
                    for b in range(2):
                        kv_job = w + 6 + 2 * b
                        act.wait_ge(kv_done, 4 * st["nth"] + 2 * b + 1)
                        for e in range(2):
                            ins = act.activation(kf[0:NOPE, 8 * b + e:8 * b + 8:2, :],
                                                 job_banks(kv_job)[NOPE * e:NOPE * e + NOPE], ACT.Copy)
                        ins.then_inc(bank_free[kv_job % 2], 1)
                        act.wait_ge(kv_done, 4 * st["nth"] + 2 * b + 2)
                        act.activation(mvt[:, :, 512 * b:512 * b + 512], job_banks(kv_job + 1, 2, 512), ACT.Copy)\
                            .then_inc(bank_free[(kv_job + 1) % 2], 1)
                        pieces(p + 20 + 2 * b, p + 22 + 2 * b)
                    scale = (NOPE + ROPE) ** -0.5
                    o0 = k.get("o")
                    act.wait_ge(qf_ready, 4 * st["nth"] + 4)
                    for n in range(HEADS + 6):
                        if n < HEADS:
                            act.wait_ge(low_ready, HEADS * st["nth"] + n + 1)
                            for a in range(2):
                                s = mp[:, n % 4, P * a:P + 2 * P * a]
                                ins = act.activation(s, s, ACT.Exp, bias=low[:, n, a:a + 1], scale=scale,
                                                     accum_out=total[:, n, a:a + 1])
                            ins.then_inc(p_ready, 1)
                        if 2 <= n < HEADS + 2:
                            h = n - 2
                            act.wait_ge(pt_done, HEADS * st["nth"] + h + 1)
                            if h >= 4:
                                act.wait_ge(o_done, o0 + (h - 4) // 2 + 1)
                            act.activation(mpt[:, h % 4, :], bk[:, 2 + h % 2, 0:384], ACT.Copy).then_inc(pt_ready, 1)
                        heads_out(n - 5)
                    pieces(p + 24, p + 28)
                    for m in range(2):
                        pieces(p + 28 + 2 * m, p + 30 + 2 * m)
                        is_done(act, c + 12 + 2 * m)
                        y_out(w + 10, m)
                    post_squares(w + 10)
                    root(w + 12)
                elif st["kind"] == "conv":
                    with act.Fori(0, 2) as i:
                        for b in range(2):
                            pieces(p + 4 + 4 * b, p + 8 + 4 * b, i)
                            is_done(act, c + 1 + 2 * b, i)
                            for e in range(2):
                                ins = act.activation(sig[:, b, e, :], job_banks(w + b)[:, e, :], ACT.Sigmoid,
                                                     bias=cols[:, bass.ds(4 * i + ROW["conv_b_pw1_2"] + KD + 2 * b + e, 1)])
                            ins.then_inc(csig_ready, 1)
                    for n in range(CONV_DVE, KD):
                        act.wait_ge(dw_done, n - CONV_DVE + 1)
                        act.activation(cacc[:, n, :], job_banks(w + 4)[:, n - CONV_DVE, :], ACT.Identity,
                                       bias=col("conv_b_dw_2", n)).then_inc(conv_act, 1)
                    act.wait_ge(conv_act, KD - CONV_DVE)
                    act.sem_inc(bank_free[w % 2], 1)
                    for q in range(4):
                        act.wait_ge(xc2_ready, q + 1)
                        squares(tmp[:, 2 * q:2 * q + 2, :], sq_pair(q), 2)
                    k.add("mean", 1)
                    root(w + 6)
                    modulate(ACT.Silu, lambda j: col("conv_ln_g_2", j), lambda j: col("conv_ln_b_2", j))
                    for m in range(2):
                        pieces(p + 20 + 4 * m, p + 24 + 4 * m)
                        is_done(act, c + 10 + 2 * m)
                        y_out(w + 5, m, "conv_b_pw2_2")
                    post_squares(w + 5)
                    root(w + 7)
                elif st["kind"] == "pool":
                    pieces(p + 4, p + 6)
                    post_squares(w)
                    root(w + 2)
                elif st["kind"] == "ffn1":
                    n = st["hid"]

                    def gated(w, slot, pair, i=0):
                        act.activation(sig[:, slot, :, :], job_banks(w, 2), ACT.Silu).then_inc(sig_ready, 1)
                        is_read(act, w, i)
                        act.activation(hid_hi[:, tiles(pair, 2), :], ev[:, slot, :, :], ACT.Copy)\
                            .then_inc(hhi_ready, 1)

                    with act.Fori(0, 4) as i:
                        for b in range(2):
                            pieces(p + 4 + 4 * b, p + 8 + 4 * b, i)
                            is_done(act, c + 1 + 2 * b, i)
                            gated(w + b, b, 2 * i + b, i)
                    for b in range(8, 11):
                        pieces(p + 4 * b + 4, p + 4 * b + 8)
                        is_done(act, c + 2 * b + 1)
                        gated(w + b, b % 2, b)
                    pieces(p + 48, p + 72)
                elif st["kind"] == "sb":
                    with act.Fori(0, 2) as i:
                        for b in range(2):
                            pieces(p + 4 + 4 * b, p + 8 + 4 * b, i)
                            is_done(act, c + 2 + 2 * b, i)
                            act.activation(qk[:, bass.ds(8 * i + 4 * b, 4), :], job_banks(w + b), ACT.Copy)\
                                .then_inc(bank_free[(w + b) % 2], 1)
                    for b in range(2):
                        pieces(p + 20 + 4 * b, p + 24 + 4 * b)
                        is_done(act, c + 10 + 2 * b)
                        act.activation(vt[:, :, 512 * b:512 * b + 512], job_banks(w + 4 + b, 2, 512), ACT.Copy)\
                            .then_inc(bank_free[(w + b) % 2], 1)
                    for n in range(HEADS + 5):
                        if n < HEADS:
                            act.wait_ge(n_ready, n + 1)
                            act.activation(sb_l[:, n % 4, :], sb_n[:, n % 4, :], ACT.Exp).then_inc(e1_ready, 1)
                            act.wait_ge(e1_ready, n + 1)
                            act.activation(sb_l[:, n % 4, :], sb_l[:, n % 4, :], ACT.Ln, bias=1.0).then_inc(l_ready, 1)
                        if 2 <= n < HEADS + 2:
                            act.wait_ge(t_ready, n - 1)
                            act.activation(sb_w[:, (n - 2) % 4, :], sb_z[:, (n - 2) % 4, :], ACT.Exp)\
                                .then_inc(e_ready, 1)
                        heads_out(n - 4)
                    pieces(p + 28, p + 36)
                elif st["kind"] == "lru":
                    for b in range(5):
                        pieces(p + 4 + 4 * b, p + 8 + 4 * b)
                        is_done(act, c + 2 + 2 * b)
                        first = 4 * b
                        for a, e, f in ((first, min(first + 4, NB), 0), (max(first, NB), first + 4, 1)):
                            if a >= e:
                                continue
                            bks = job_banks(w + b)[:, a - first:e - first, :]
                            if f:
                                ins = act.activation(lxb[:, a - NB:e - NB, TAPS - 1:], bks, ACT.Copy)
                            else:
                                ins = act.activation(lg[:, a:e, :], bks, ACT.Gelu_apprx_tanh)
                        ins.then_inc(bank_free[(w + b) % 2], 1)
                        for n in range(max(first - NB, 0), first + 4 - NB):
                            if n == 0:
                                act.wait_ge(xb_zero, 1)
                            is_read(act, w + b)
                            act.activation(lxc[:, n, :], lxb[:, n, 0:S], ACT.Identity,
                                           bias=col("lru_conv_b", n), scale=col("lru_conv_w", n)).then_inc(xc_first, 1)
                    for n in range(NB):
                        act.wait_ge(ri_done, n + 1)
                        act.activation(lri[:, n, 0, :], bk[:, n % 8, 0:S], ACT.Sigmoid, bias=col("lru_b_r", n))
                        act.activation(lri[:, n, 1, :], bk[:, n % 8, S:2 * S], ACT.Sigmoid, bias=col("lru_b_i", n))\
                            .then_inc(ri_ready, 1)
                    for n in range(NB):
                        act.wait_ge(ri_ready, n + 1)
                        act.activation(lxb[:, n, 0:S], lri[:, n, 0, :], ACT.Exp, scale=lsp[:, 4, n:n + 1])
                        act.activation(lru_t(n), lri[:, n, 0, :], ACT.Tanh, scale=lsp[:, 5, n:n + 1])\
                            .then_inc(a_ready, 1)
                    for n in range(NB):
                        act.wait_ge(v_ready, n + 1)
                        act.activation(lri[:, n, 0, :], lri[:, n, 0, :], ACT.Sqrt).then_inc(s_ready, 1)
                    pieces(p + 24, p + 36)

            if len(stages) <= 6:
                final_norm(W_END)

        @block.tensor
        def _(pe):
            k = Counts()
            pe.sem_inc(piece_used, OPS)

            def piece(p, i, ready, xs, kt, outs, first, last):
                if ready is not None:
                    pe.wait_ge(*ready)
                pe.wait_ge(lo_ready, 2 * RAWS + p + 1 + 8 * i)
                n = 2
                for r in range(n):
                    wh, wl = (z[:, p % OPS, 512 * r:512 * r + 512] for z in (w_hi, w_lo))
                    xh, xl = (z(kt + r) for z in xs)
                    f, l = first and r == 0, last and r == n - 1
                    ins = outs(wh, wl, xh, xl, f, l)
                ins.then_inc(piece_used, 2 if p in double else 1)

            def by_feature(w):
                def go(wh, wl, xh, xl, first, last):
                    for m in range(4):
                        o = job_banks(w)[:, m, :]
                        s = slice(P * m, P * m + P)
                        pe.matmul(o, wh[:, s], xh, start=first, stop=False)
                        pe.matmul(o, wh[:, s], xl, start=False, stop=False)
                        ins = pe.matmul(o, wl[:, s], xh, start=False, stop=last)
                    return ins
                return go

            def by_token(w):
                def go(wh, wl, xh, xl, first, last):
                    for b in range(2):
                        o = job_banks(w, 2, 512)[:, b, :]
                        s = slice(P * b, P * b + P)
                        pe.matmul(o, xh[:, s], wh, start=first, stop=False)
                        pe.matmul(o, xh[:, s], wl, start=False, stop=False)
                        ins = pe.matmul(o, xl[:, s], wh, start=False, stop=last)
                    return ins
                return go

            def job(c, w, i, xs, kt0, kts, ready, outs=None, second=None):
                is_free(pe, w, i)
                n = (kts + 1) // 2
                for q in range(n):
                    piece(2 * c + q, i, ready(q) if ready else None, xs, kt0 + 2 * q, outs or by_feature(w),
                          q == 0, q == n - 1)
                    if second is not None and q == 0:
                        second()

            def gate_up(c, w, i, act_from=None):
                is_free(pe, w, i)
                for q in range(4):
                    p = 2 * c + q
                    pe.wait_ge(lo_ready, 2 * RAWS + p + 1 + 8 * i)
                    for r in range(4):
                        f = q % 2 * 4 + r
                        if act_from is not None and q < 2 and f % 2 == 0:
                            pe.wait_ge(act_ready, act_from + f // 2 + 1)
                        for m in range(2):
                            o = job_banks(w)[:, q // 2 * 2 + m, :]
                            wh, wl = (z[:, p % OPS, 256 * r + P * m:256 * r + P * m + P] for z in (w_hi, w_lo))
                            pe.matmul(o, wh, a_hi[:, f, :], start=(f == 0), stop=False)
                            pe.matmul(o, wh, a_lo[:, f, :], start=False, stop=False)
                            ins = pe.matmul(o, wl, a_hi[:, f, :], start=False, stop=(f == KD - 1))
                    ins.then_inc(piece_used, 1)

            def mean(w, src, n, ready=None):
                is_free(pe, w)
                for j in range(n):
                    if ready is not None:
                        ready(j)
                    elif j % 2 == 0:
                        pe.wait_ge(sq_ready, k.next("sq") + 1)
                    ins = pe.matmul(job_flat(w, S), ones[:, :], src(j), start=(j == 0), stop=(j == n - 1))
                ins.then_inc(mean_done, 1)
                k.add("root", 1)

            def y_mean(w):
                mean(w, lambda j: sq_pair(j // 2)[:, j % 2, :], KD)

            def x_mean(w):
                mean(w, lambda j: tmp[:, j, :], KD)

            def head_out(h, v, wt, ready):
                m, r = h // 2, slice(DH * (h % 2), DH * (h % 2) + DH)
                pe.wait_ge(*ready)
                if h % 2 == 0 and m >= 2:
                    pe.wait_ge(oact_ready, k.get("oact") + m - 1)
                o = bk[r, 4 + m % 2, :]
                pe.matmul(o[:, 0:S], v[:, 0, DH * h:DH * h + DH], wt[:, 0:S], start=True, stop=False)
                ins = pe.matmul(o[:, P:S], v[:, 1, DH * h:DH * h + DH], wt[:, S:384], start=False, stop=True)
                if h % 2:
                    ins.then_inc(o_done, 1)
                if h == HEADS - 1:
                    k.add("oact", HEADS // 2)

            def turn(w, blocks):
                is_free(pe, w)
                for j, b in enumerate(blocks):
                    r = b.shape[0]
                    ins = pe.transpose(job_flat(w, 2048)[:, P * j:P * j + r], b, ident[0:r, 0:r])
                ins.then_inc(turn_done, 1)
                k.add("turn", 1)

            def mod_sum(g, w, a=0, b=MODC // P):
                if a == 0:
                    is_free(pe, w)
                    pe.wait_ge(mod_used, 2 + UNITS * (g + 1))
                for j in range(a, b):
                    ins = pe.matmul(job_flat(w, MODC // P)[:, j:j + 1], mod_acc[:, P * j:P * j + P], one1[:, 0:1],
                                    start=True, stop=True)
                if b == MODC // P:
                    ins.then_inc(turn_done, 1)
                    k.add("turn", 1)

            def turned():
                pe.wait_ge(turn_read, k.get("turn"))

            pe.wait_ge(consts, 4)
            pe.wait_ge(loaded, 16 * NLOADS)
            turn(0, [xin[:, b, P * j:P * j + P] for j in range(KD) for b in range(2)])
            turn(1, [rows[0:min(P, NROW - P * j), j, :] for j in range(NPT)])
            turned()
            pe.wait_ge(pos_ready, 1)
            for j in range(2):
                pe.matmul(bk[:, 0, j:j + 1], rrow[:, j, :], one1[0:1, 0:1], start=True, stop=True)
            pe.matmul(bk[:, 1, 0:S], one1[0:1, :], pos_f[:, :], start=True, stop=True).then_inc(rope_in, 1)
            pe.wait_ge(rope_read, 1)
            mod_sum(0, 0)
            turned()

            for st in stages:
                c, w, g = st["c"], st["w"], st["n"]
                A = (y_hi, y_lo)
                H = (lambda f: hid_hi[:, f, :], lambda f: hid_lo[:, f, :])
                if g == 6:
                    x_mean(w)
                if st["late"]:
                    mod_sum(st["late"], w + 1, 0, 10)
                x_mean(w)
                if st["late"]:
                    mod_sum(st["late"], w + 1, 10)
                    turned()
                nq = act_base[g]
                act_in = lambda q: (act_ready, nq + q + 1)
                if st["kind"] == "ffn2":
                    with pe.Fori(0, 4) as i:
                        for b in range(2):
                            gate_up(c + 2 * b, w + b, i, nq)
                    for m in range(2):
                        job(c + 16 + 8 * m, w + 8 + m, 0, H, 0, F2 // P,
                            (lambda q: (hid_ready, 2 + st["hid"] + q + 1)) if m == 0 else None,
                            second=(lambda: mod_sum(st["groups"][0], w + 9)) if m == 0 and st["groups"] else None)
                        turned()
                    y_mean(w + 10)
                elif st["kind"] == "mla":
                    C = (lambda f: cn_hi[:, f, :], lambda f: cn_lo[:, f, :])
                    nc_ = 3 * st["nth"]

                    def by_columns(w, starts):
                        def go(p, r, f, xs, first, last):
                            wh, wl = (z[:, p % OPS, :] for z in (w_hi, w_lo))
                            xh, xl = (z(f) for z in xs)
                            for m, a in enumerate(starts(r)):
                                o = job_banks(w)[:, m, :]
                                pe.matmul(o, wh[:, a:a + P], xh, start=first, stop=False)
                                pe.matmul(o, wh[:, a:a + P], xl, start=False, stop=False)
                                ins = pe.matmul(o, wl[:, a:a + P], xh, start=False, stop=last)
                            return ins
                        return go

                    for n, (width, starts) in enumerate(((QL, (0, P, 2 * P)), (KVL + 2 * ROPE, (0, P, KVL - NOPE)))):
                        is_free(pe, w + n)
                        go = by_columns(w + n, lambda r: [r * width + a for a in starts])
                        for q in range(4):
                            p = 2 * (c + 2 * n) + q
                            if n == 0:
                                pe.wait_ge(*act_in(q))
                            pe.wait_ge(lo_ready, 2 * RAWS + p + 1)
                            for r in range(2):
                                ins = go(p, r, 2 * q + r, A, q == 0 and r == 0, q == 3 and r == 1)
                            ins.then_inc(piece_used, 1)
                    mean(w + 2, lambda j: sq_pair(j // 2)[:, j % 2, :], 3)
                    mean(w + 3, lambda j: sq_pair(2)[:, j, :], 2)
                    for b in range(4):
                        is_free(pe, w + 2 + b)
                        if b == 1:
                            pe.wait_ge(rms_ready, k.get("root"))
                        go = by_columns(w + 2 + b, lambda r: [r * 512 + P * m for m in range(4)])
                        for q in range(2):
                            p = 2 * (c + 4 + b) + q
                            if b == 0:
                                pe.wait_ge(cn_ready, nc_ + q + 1)
                            pe.wait_ge(lo_ready, 2 * RAWS + p + 1)
                            for r in range(2 - q):
                                ins = go(p, r, 2 * q + r, C, q == 0 and r == 0, q == 1)
                            ins.then_inc(piece_used, 1)
                    pe.wait_ge(cn_ready, nc_ + 3)
                    for b in range(2):
                        p = 2 * (c + 8 + b)
                        j = w + 6 + 2 * b
                        is_free(pe, j)
                        for r in range(2):
                            pe.wait_ge(lo_ready, 2 * RAWS + p + r + 1)
                            wh, wl = (z[:, (p + r) % OPS, :] for z in (w_hi, w_lo))
                            xh, xl = (z(3 + r) for z in C)
                            for m in range(4):
                                o, s = job_banks(j)[:, m, :], slice(P * m, P * m + P)
                                pe.matmul(o, wh[:, s], xh, start=(r == 0), stop=False)
                                pe.matmul(o, wh[:, s], xl, start=False, stop=False)
                                ins = pe.matmul(o, wl[:, s], xh, start=False, stop=(r == 1))
                        ins.then_inc(kv_done, 1)
                        is_free(pe, j + 1)
                        for a in range(2):
                            for r in range(2):
                                wh, wl = (z[:, (p + r) % OPS, 512:] for z in (w_hi, w_lo))
                                xh, xl = (z(3 + r)[:, P * a:P * a + P] for z in C)
                                o = job_banks(j + 1, 2, 512)[:, a, :]
                                pe.matmul(o, xh, wh, start=(r == 0), stop=False)
                                pe.matmul(o, xh, wl, start=False, stop=False)
                                ins = pe.matmul(o, xl, wh, start=False, stop=(r == 1))
                        ins.then_inc(kv_done, 1)
                        pe.wait_ge(kv_done, 4 * st["nth"] + 2 * b + 2)
                        pe.sem_inc(piece_used, 2)
                    for j in (w + 8, w + 9):
                        is_read(pe, j)
                    pe.wait_ge(qf_ready, 4 * st["nth"] + 4)
                    pe.wait_ge(kr_ready, st["nth"] + 1)
                    n0 = HEADS * st["nth"]
                    for n in range(HEADS + 4):
                        if n < HEADS:
                            if n >= 2:
                                pe.wait_ge(sm_ready, n0 + n - 1)
                            r = slice(0, NOPE + ROPE)
                            pe.matmul(bk[:, n % 2, 0:P], qf[r, n, 0:P], kf[r, n, 0:P], start=True, stop=True)
                            pe.matmul(bk[:, n % 2, P:384], qf[r, n, P:S], kf[r, n, :], start=True, stop=True)\
                                .then_inc(s_done, 1)
                        if 2 <= n < HEADS + 2:
                            h = n - 2
                            pe.wait_ge(pn_ready, n0 + h + 1)
                            if h >= 2:
                                pe.wait_ge(pt_ready, n0 + h - 1)
                            for a in range(3):
                                ins = pe.transpose(bk[:, 2 + h % 2, P * a:P * a + P], mp[:, h % 4, P * a:P * a + P],
                                                   ident[:, :])
                            ins.then_inc(pt_done, 1)
                        if n >= 4:
                            h = n - 4
                            head_out(h, mvt, mpt[:, h % 4, :], (pt_ready, n0 + h + 1))
                    pe.wait_ge(oact_ready, k.get("oact"))
                    for m in range(2):
                        job(c + 10 + 2 * m, w + 10 + m, 0, A, 0, KD, None)
                    y_mean(w + 12)
                elif st["kind"] == "conv":
                    with pe.Fori(0, 2) as i:
                        for b in range(2):
                            gate_up(c + 2 * b, w + b, i, nq)

                    def convolved(j):
                        if j < CONV_DVE:
                            pe.wait_ge(conv_dve, j + 1)
                        else:
                            pe.wait_ge(conv_act, j - CONV_DVE + 1)
                    is_free(pe, w + 4)
                    for n in range(CONV_DVE, KD):
                        if n % 2 == 0 or n == CONV_DVE:
                            is_read(pe, w + n // 2)
                        pe.wait_ge(diag_ready, n - CONV_DVE + 1)
                        for tap in range(WIDTH):
                            ins = pe.matmul(job_banks(w + 4)[:, n - CONV_DVE, :], diag[:, n - CONV_DVE, tap, :],
                                            cu[:, n, tap:tap + S], start=(tap == 0), stop=(tap == WIDTH - 1))
                        ins.then_inc(dw_done, 1)
                    mean(w + 5, lambda j: cacc[:, j, :], KD, convolved)
                    k.add("root", -1)
                    y_mean(w + 6)
                    for m in range(2):
                        job(c + 8 + 2 * m, w + 5 + m, 0, A, 0, KD, (lambda q: (act_ready, nq + 4 + q + 1)) if m == 0 else None)
                    y_mean(w + 7)
                elif st["kind"] == "pool":
                    for m in range(2):
                        is_free(pe, w + m)
                        for r in range(2):
                            pe.wait_ge(lo_ready, 2 * RAWS + 2 * c + r + 1)
                            wh, wl = (z[:, (2 * c + r) % OPS, :] for z in (w_hi, w_lo))
                            for e in range(4):
                                g_ = 2 * m + e // 2
                                if m == 0 and r == 0 or e % 2 == 0:
                                    pe.wait_ge(act_ready, nq + g_ + 1)
                                o, s = job_banks(w + m)[:, e, :], slice(256 * g_ + P * (e % 2), 256 * g_ + P * (e % 2) + P)
                                xh, xl = a_hi[:, 2 * g_ + r, :], a_lo[:, 2 * g_ + r, :]
                                pe.matmul(o, wh[:, s], xh, start=(r == 0), stop=False)
                                pe.matmul(o, wh[:, s], xl, start=False, stop=False)
                                ins = pe.matmul(o, wl[:, s], xh, start=False, stop=(r == 1))
                        ins.then_inc(pool_done, 1)
                    pe.wait_ge(pool_done, 2)
                    pe.sem_inc(piece_used, 2)
                    y_mean(w + 2)
                elif st["kind"] == "ffn1":
                    with pe.Fori(0, 4) as i:
                        for b in range(2):
                            gate_up(c + 2 * b, w + b, i, nq)
                    for b in range(8, 11):
                        gate_up(c + 2 * b, w + b, 0)
                    for m in range(2):
                        job(c + 22 + 6 * m, w + 11 + m, 0, H, 0, 22,
                            (lambda q: (hid_ready, 2 + st["hid"] + q + 1)) if m == 0 else None,
                            second=(lambda: mod_sum(st["groups"][0], w + 12)) if m == 0 else None)
                        turned()
                elif st["kind"] == "sb":
                    with pe.Fori(0, 2) as i:
                        for b in range(2):
                            job(c + 2 * b, w + b, i, A, 0, KD, act_in)
                    for b in range(2):
                        job(c + 8 + 2 * b, w + 4 + b, 0, A, 0, KD, None, by_token(w + 4 + b))
                    is_read(pe, w + 4)
                    is_read(pe, w + 5)
                    for n in range(HEADS + 3):
                        if n < HEADS:
                            m, r = n // 2, slice(DH * (n % 2), DH * (n % 2) + DH)
                            if n >= 2:
                                pe.wait_ge(z_copied, n - 1)
                            pe.matmul(bk[:, n % 2, 0:S], qk[r, KD + m, 0:P], qk[r, m, :], start=True, stop=True)
                            pe.matmul(bk[:, n % 2, S:384], qk[r, KD + m, P:S], qk[r, m, P:S], start=True, stop=True)\
                                .then_inc(z_done, 1)
                        if 1 <= n <= HEADS:
                            h = n - 1
                            pe.wait_ge(spm_ready, h + 1)
                            if h >= 2:
                                pe.wait_ge(t_ready, h - 1)
                            o, s = bk[:, 2 + h % 2, :], sb_s[:, h % 4, :]
                            pe.matmul(o[:, 0:S], tri[:, :], s[:, 0:S], start=True, stop=False)
                            pe.matmul(o[:, P:S], one1[:, :], s[:, S:384], start=False, stop=True)
                            pe.matmul(o[:, S:384], tri[:, :], s[:, S:384], start=True, stop=True).then_inc(suf_done, 1)
                        if n >= 3:
                            h = n - 3
                            head_out(h, vt, sb_w[:, h % 4, :], (w_ready, h + 1))
                    pe.wait_ge(oact_ready, HEADS // 2)
                    for m in range(2):
                        job(c + 12 + 2 * m, w + 6 + m, 0, A, 0, KD, None)
                elif st["kind"] == "lru":
                    for b in range(5):
                        job(c + 2 * b, w + b, 0, A, 0, KD, act_in if b == 0 else None)
                    is_read(pe, w + 3)
                    is_read(pe, w + 4)
                    pe.wait_ge(lw_landed, 32)
                    for n in range(NB):
                        pe.wait_ge(xc_ready, n + 1)
                        if n >= 8:
                            pe.wait_ge(ri_ready, n - 7)
                        pe.matmul(bk[:, n % 8, 0:S], lw[:, n, :], lxc[:, n, :], start=True, stop=True)
                        pe.matmul(bk[:, n % 8, S:2 * S], lw[:, NB + n, :], lxc[:, n, :], start=True, stop=True)\
                            .then_inc(ri_done, 1)
                    pe.wait_ge(ri_ready, NB)
                    for m in range(2):
                        job(c + 10 + 3 * m, w + 5 + m, 0, A, 0, NB,
                            (lambda q: (lact_ready, 2 * q + 2)) if m == 0 else None)
            if len(stages) <= 6:
                x_mean(W_END)
            pe.wait_ge(x_done, 4 + 4 * max(0, len(stages) - 6))
            for b in range(2):
                is_free(pe, W_END + b)
                for j in range(KD):
                    ins = pe.transpose(job_flat(W_END + b, D)[:, P * j:P * j + P], x[:, j, P * b:P * b + P], ident[:, :])
                ins.then_inc(turn_done, 1)

        @block.vector
        def _(dve):
            k = Counts()
            dve.sem_inc(lo_ready, 2 * RAWS)
            dve.sem_inc(mod_used, 2)
            dve.sem_inc(hid_ready, 2)

            def own(ins):
                ins.then_inc(dve_step, 1)
                return k.next("step") + 1

            def own_wait(n):
                dve.wait_ge(dve_step, n)

            def pieces(a, b, i=0):
                for p in range(a, b):
                    c = p // 2
                    if p >= NPIECE or p - 1 in double:
                        continue
                    dve.wait_ge(hi_ready, p + 1 + 8 * i)
                    for o, r in split(p):
                        ins = dve.tensor_tensor(o(w_lo[:, p % OPS, :]), r(raw[:, c % RAWS, :]),
                                                o(w_hi[:, p % OPS, :].bitcast(F32)), ALU.subtract)
                    ins.then_inc(lo_ready, 2 if p in double else 1)

            def mod_add(g, i, u):
                cc = cact[:, 0:KD] if g < 6 else cact[:, KD:2 * KD]
                dve.wait_ge(mod_landed[u % 2], 16 * (UNITS // 2 * g + 2 * i + u // 2 + 1))
                dve.wait_ge(mod_used, UNITS * g + 4 * i + u + 1)
                a = mod_acc[:, u % 2 * MODW:(u % 2 + 1) * MODW]
                if isinstance(i, int) and i == 0 and u < 2:
                    dve.tensor_scalar(a, mod_raw[:, u % 2, :], cc[:, 0:1], None, ALU.mult).then_inc(mod_used, 1)
                    return
                dve.scalar_tensor_tensor(out=a, in0=mod_raw[:, u % 2, :], scalar=cc[:, bass.ds(2 * i + u // 2, 1)],
                                         in1=a, op0=ALU.mult, op1=ALU.add).then_inc(mod_used, 1)

            def turn_in(dst, w, n):
                dve.wait_ge(turn_done, k.next("turn") + 1)
                dve.tensor_copy(dst, job_flat(w, n)).then_inc(turn_read, 1)

            def mod_finish(g, w):
                dve.wait_ge(turn_done, k.next("turn") + 1)
                dve.tensor_tensor(mv[:, g, :], job_flat(w, MODC // P), mod_bias(g), ALU.add).then_inc(turn_read, 1)
                dve.wait_ge(turn_read, k.get("turn"))
                gain = col("norm_g", 8 * g, 8) if g < 6 else col("norm_g_2", 16 * (g - 6), 8)
                dve.scalar_tensor_tensor(out=mv_a[:, g, :], in0=mv[:, g, 8:16], scalar=1.0, in1=gain,
                                         op0=ALU.add, op1=ALU.mult)
                gate = mv[:, g, 16:24]
                if g >= 6:
                    ins = dve.tensor_tensor(mv_g[:, g, :], gate, col("norm_g_2", 16 * (g - 6) + 8, 8), ALU.mult)
                elif g % 3 == 1:
                    ins = dve.tensor_scalar(mv_g[:, g, :], gate, 1.0, None, ALU.add)
                else:
                    ins = dve.tensor_scalar(mv_g[:, g, :], gate, 1.0, 0.5, ALU.add, ALU.mult)
                ins.then_inc(mod_ready, 1)

            def inverse():
                s = k.get("rms") % 2
                dve.wait_ge(rms_ready, k.next("rms") + 1)
                own_wait(own(dve.reciprocal(inv[:, s, :], rms[:, s, :])))
                return inv[:, s, :]

            def normed(src, dst, n, ready, iv):
                for q in range(0, n, 2):
                    e = min(q + 2, n)
                    dve.tensor_tensor(dst[:, q:e, :], src[:, q:e, :], iv.unsqueeze(1).to_broadcast([P, e - q, S]),
                                      ALU.mult).then_inc(ready, 1)

            def final_norm():
                iv = inverse()
                for j in range(KD):
                    ins = dve.scalar_tensor_tensor(out=x[:, j, :], in0=x[:, j, :], scalar=col("final_norm_g", j),
                                                   in1=iv, op0=ALU.mult, op1=ALU.mult)
                    if j % 2:
                        ins.then_inc(x_done, 1)

            def post(g, w):
                iv = inverse()
                step = [own(dve.tensor_tensor(tmp[:, 2 * q:2 * q + 2, :], tmp[:, 2 * q:2 * q + 2, :],
                                              iv.unsqueeze(1).to_broadcast([P, 2, S]), ALU.mult)) for q in range(4)]
                for j in range(KD):
                    if j % 2 == 0:
                        own_wait(step[j // 2])
                    ins = dve.scalar_tensor_tensor(out=x[:, j, :], in0=tmp[:, j, :], scalar=mv_g[:, g, j:j + 1],
                                                   in1=x[:, j, :], op0=ALU.mult, op1=ALU.add)
                    if j % 2:
                        ins.then_inc(x_done, 1)

            def heads_out(n):
                if n >= 0 and n % 2 == 0 and n // 2 < HEADS // 2:
                    m = n // 2
                    dve.wait_ge(ohi_ready, k.next("ohi") + 1)
                    dve.tensor_tensor(a_lo[:, m, :], bk[:, 4 + m % 2, 0:S], a_hi[:, m, :].bitcast(F32),
                                      ALU.subtract).then_inc(oact_ready, 1)

            def act_high():
                for q in range(4):
                    dve.wait_ge(h_ready, k.next("h") + 1)
                    dve.tensor_copy(a_hi[:, 2 * q:2 * q + 2, :], tmp[:, 2 * q:2 * q + 2, :]).then_inc(ahi_ready, 1)

            def residual(w, c, m, g):
                is_done(dve, c)
                for j in range(4):
                    f = 4 * m + j
                    ins = dve.scalar_tensor_tensor(out=x[:, f, :], in0=job_banks(w)[:, j, :],
                                                   scalar=mv_g[:, g, f:f + 1], in1=x[:, f, :],
                                                   op0=ALU.mult, op1=ALU.add)
                ins.then_inc(bank_free[w % 2], 1)

            dve.wait_ge(pos_landed, 16)
            dve.tensor_copy(pos_f[:, :], pos_i[:, :]).then_inc(pos_ready, 1)
            turn_in(x[:, :, :].rearrange("p k s -> p (k s)"), 0, 2048)
            turn_in(cols[:, 0:NROW], 1, NROW)
            dve.wait_ge(turn_read, 2)
            dve.wait_ge(cact_ready, 2)
            u, r, r2, s = (lsp[:, j, :] for j in (1, 2, 3, 0))
            own_wait(own(dve.tensor_scalar(r, u, 2.0, None, ALU.add)))
            own_wait(own(dve.reciprocal(r2, r)))
            own_wait(own(dve.tensor_tensor(r, u, r2, ALU.mult)))
            own_wait(own(dve.tensor_tensor(r2, r, r, ALU.mult)))
            own_wait(own(dve.tensor_scalar(s, r2, 1.0 / 17, 1.0 / 15, ALU.mult, ALU.add)))
            for d in (13, 11, 9, 7, 5, 3, 1):
                own_wait(own(dve.tensor_tensor(s, s, r2, ALU.mult)))
                own_wait(own(dve.tensor_scalar(s, s, 1.0 / d, None, ALU.add)))
            own_wait(own(dve.scalar_tensor_tensor(out=s, in0=s, scalar=2.0, in1=r, op0=ALU.mult, op1=ALU.mult)))
            own_wait(own(dve.tensor_scalar(r, col("lru_lambda", 0, NB), -1.0, 0.0, ALU.mult, ALU.max)))
            own_wait(own(dve.tensor_tensor(s, s, r, ALU.add)))
            dve.tensor_scalar(lsp[:, 4, :], s, -8.0, None, ALU.mult)
            dve.tensor_scalar(lsp[:, 5, :], s, 8.0, None, ALU.mult)
            dve.wait_ge(rope_in, 1)
            own_wait(own(dve.tensor_copy(rcol[:, :], bk[:, 0, 0:2])))
            ang, tr, red = ev[:, 0, 0, :], ev[:, 0, 1, :], ev[:, 1, 0, :]
            dve.tensor_scalar(ang, bk[:, 1, 0:S], rcol[:, 0:1], None, ALU.mult).then_inc(rope_read, 1)
            dve.wait_ge(rope_read, 1)
            own_wait(own(dve.tensor_scalar(turns_i[:, :], ang, 1.0 / (2 * np.pi), None, ALU.mult)))
            own_wait(own(dve.tensor_copy(tr, turns_i[:, :])))
            parts = two_pi_parts()
            for n, cst in enumerate(parts):
                own_wait(own(dve.scalar_tensor_tensor(out=red if n % 2 == 0 else ang, in0=tr, scalar=-cst,
                                                      in1=ang if n % 2 == 0 else red, op0=ALU.mult, op1=ALU.add)))
            own_wait(own(dve.tensor_scalar(ang, red, 3.1415925, -3.1415925, ALU.min, ALU.max)))
            own_wait(own(dve.tensor_scalar(red, ang, -1.0, None, ALU.mult)))
            own_wait(own(dve.tensor_tensor(tr, ang, red, ALU.min)))
            own_wait(own(dve.tensor_scalar(red, ang, rcol[:, 1:2], None, ALU.mult)))
            dve.tensor_copy(ev[NOPE + ROPE:P, 0, 0, :], ev[NOPE + ROPE:P, 1, 0, :])
            dve.tensor_scalar(ev[NOPE:NOPE + ROPE, 0, 0, :], ev[NOPE:NOPE + ROPE, 0, 1, :], float(np.pi / 2), None, ALU.add)\
                .then_inc(rope_arg, 1)

            def added(i):
                for u in range(4):
                    mod_add(0, i, u)

            added(0)
            with dve.Fori(1, 4) as i:
                added(i)
            mod_finish(0, 0)
            pieces(0, 4)

            for st in stages:
                p, c, w, g = 2 * st["c"], st["c"], st["w"], st["n"]
                if g == 6:
                    final_norm()
                normed(x, tmp, KD, xn_ready, inverse())
                if st["kind"] != "pool":
                    act_high()
                if st["late"]:
                    mod_finish(st["late"], w + 1)
                if st["kind"] == "ffn2":
                    n = st["hid"]

                    def two_jobs(i):
                        for b in range(2):
                            for u in range(2 * b, 2 * b + 2):
                                pieces(p + 4 + 2 * u, p + 6 + 2 * u, i)
                                if st["groups"]:
                                    mod_add(st["groups"][0], i, u)
                            for e in range(2):
                                dve.wait_ge(sig_ready, n + 2 * b + e + 1 + 4 * i)
                                dve.wait_ge(hid_ready, n + 2 * b + e + 1 + 4 * i)
                                dve.tensor_tensor(ev[:, e, :, :], sig[:, e, :, :], sig[:, e, :, :], ALU.mult)\
                                    .then_inc(bank_free[(w + b) % 2] if e else prod_ready, 1)

                    two_jobs(0)
                    with dve.Fori(1, 4) as i:
                        two_jobs(i)
                    if st["groups"]:
                        mod_finish(st["groups"][0], w + 9)
                    for u in range(UNITS):
                        pieces(p + 36 + 2 * u, p + 38 + 2 * u)
                        if len(st["groups"]) > 1:
                            mod_add(st["groups"][1], u // 4, u % 4)
                    post(g, w + 8)
                elif st["kind"] == "mla":
                    pieces(p + 4, p + 12)
                    def rotate(src, a, b, last):
                        n = src.shape[1]
                        tab = lambda r: rope[r, :].unsqueeze(1).to_broadcast([ROPE, n, S])
                        C_, S_ = slice(NOPE, NOPE + ROPE), slice(NOPE + ROPE, P)
                        own(dve.tensor_tensor(a, src[C_], tab(C_), ALU.mult))
                        dve.tensor_tensor(b, src[S_], tab(S_), ALU.mult).then_inc(*last)

                    dve.wait_ge(ckv_out, st["nth"] + 1)
                    dve.wait_ge(rope_ready, 1)
                    R = slice(NOPE, NOPE + ROPE)
                    a, b_, kr = ev[R, 1, 0:1, :], ev[R, 1, 1:2, :], sig[R, 1, 1:2, :]
                    rotate(job_banks(w + 1)[:, 2:3, :], a, b_, (bank_free[(w + 1) % 2], 1))
                    own_wait(k.get("step"))
                    is_read(dve, w + 1)
                    own_wait(own(dve.tensor_tensor(kr, a, b_, ALU.add)))
                    dve.tensor_copy(kf[R, :, :], kr.to_broadcast([ROPE, HEADS, S])).then_inc(kr_ready, 1)
                    for a0, name, first, count in (("q", "mla_q_norm_g_2", 0, 3), ("kv", "mla_kv_norm_g_2", 3, 2)):
                        iv = inverse()
                        step = []
                        for j in range(count):
                            step.append(own(dve.scalar_tensor_tensor(
                                out=cn[:, first + j, :], in0=cn[:, first + j, :], scalar=col(name, count * st["nth"] + j),
                                in1=iv, op0=ALU.mult, op1=ALU.mult)))
                        own_wait(step[-1])
                        for j in range(0, count, 2):
                            e = min(j + 2, count)
                            dve.tensor_copy(cn_hi[:, first + j:first + e, :], cn[:, first + j:first + e, :])\
                                .then_inc(cnh_ready, 1)
                    for b in range(4):
                        pieces(p + 12 + 2 * b, p + 14 + 2 * b)
                        dve.wait_ge(nope_out, 4 * st["nth"] + b + 1)
                        if b:
                            dve.wait_ge(qf_ready, 4 * st["nth"] + b)
                        rotate(job_banks(w + 2 + b), tmp[R, 0:4, :], tmp[R, 4:8, :], (bank_free[(w + b) % 2], 1))
                        own_wait(k.get("step"))
                        is_read(dve, w + 2 + b)
                        dve.tensor_tensor(qf[R, 4 * b:4 * b + 4, :], tmp[R, 0:4, :], tmp[R, 4:8, :], ALU.add)\
                            .then_inc(qf_ready, 1)
                    pieces(p + 20, p + 24)
                    dve.wait_ge(seen_ready, st["nth"] + 1)
                    n0 = HEADS * st["nth"]
                    for n in range(HEADS + 7):
                        if n < HEADS:
                            dve.wait_ge(s_done, n0 + n + 1)
                            if n >= 4:
                                dve.wait_ge(pt_done, n0 + n - 3)
                            dve.tensor_tensor(mp[:, n % 4, :], bk[:, n % 2, 0:384], seen[:, :], ALU.add).then_inc(sm_ready, 1)
                            dve.wait_ge(sm_ready, n0 + n + 1)
                            for a in range(2):
                                ins = dve.tensor_reduce(top[:, n, a:a + 1], mp[:, n % 4, P * a:P + 2 * P * a], AX_X, ALU.max)
                            own_wait(own(ins))
                            dve.tensor_scalar(low[:, n, :], top[:, n, :], -(NOPE + ROPE) ** -0.5, None, ALU.mult)\
                                .then_inc(low_ready, 1)
                        if 1 <= n <= HEADS:
                            dve.wait_ge(p_ready, n0 + n)
                            dve.reciprocal(part[:, n - 1, :], total[:, n - 1, :]).then_inc(part_ready, 1)
                        heads_out(n - 6)
                    pieces(p + 24, p + 32)
                    post(g, w + 10)
                elif st["kind"] == "conv":
                    dve.wait_ge(cu_zero, 1)
                    with dve.Fori(0, 2) as i:
                        for b in range(2):
                            pieces(p + 4 + 4 * b, p + 8 + 4 * b, i)
                            is_done(dve, c + 2 + 2 * b, i)
                            dve.wait_ge(csig_ready, b + 1 + 2 * i)
                            for e in range(2):
                                ins = dve.scalar_tensor_tensor(
                                    out=cu[:, bass.ds(4 * i + 2 * b + e, 1), WIDTH - 1:],
                                    in0=job_banks(w + b)[:, 2 + e:3 + e, :],
                                    scalar=cols[:, bass.ds(4 * i + ROW["conv_b_pw1_2"] + 2 * b + e, 1)],
                                    in1=sig[:, b, e:e + 1, :], op0=ALU.add, op1=ALU.mult)
                            ins.then_inc(bank_free[(w + b) % 2], 1)
                    step = {}
                    for tap in range(WIDTH):
                        for n in range(CONV_DVE):
                            if tap == 0:
                                if n % 2 == 0:
                                    is_read(dve, w + n // 2)
                                ins = dve.tensor_scalar(cacc[:, n, :], cu[:, n, 0:S], col("conv_w_dw_2", n),
                                                        col("conv_b_dw_2", n), ALU.mult, ALU.add)
                            else:
                                own_wait(step[n])
                                ins = dve.scalar_tensor_tensor(out=cacc[:, n, :], in0=cu[:, n, tap:tap + S],
                                                               scalar=col("conv_w_dw_2", KD * tap + n),
                                                               in1=cacc[:, n, :], op0=ALU.mult, op1=ALU.add)
                            if tap < WIDTH - 1:
                                step[n] = own(ins)
                            else:
                                ins.then_inc(conv_dve, 1)
                    dve.wait_ge(mean_done, MEAN_CONV)
                    for q in range(4):
                        dve.tensor_tensor(tmp[:, 2 * q:2 * q + 2, :], cacc[:, 2 * q:2 * q + 2, :],
                                          job_flat(w + 5, S).unsqueeze(1).to_broadcast([P, 2, S]), ALU.subtract)\
                            .then_inc(xc2_ready, 1)
                    iv = inverse()
                    normed(tmp, tmp, KD, xn_ready, iv)
                    act_high()
                    pieces(p + 20, p + 28)
                    post(g, w + 5)
                elif st["kind"] == "pool":
                    for _ in range(4):
                        dve.wait_ge(h_ready, k.next("h") + 1)
                    src, dst = ph, pa
                    step = None
                    for lv, win in enumerate(WINDOWS):
                        f = 2 * lv
                        if step is not None:
                            own_wait(step)
                        step = own(dve.tensor_tensor(dst[:, f:, win - 1:], src[:, f:, win - 1:],
                                                     src[:, f:, win - 1 - win // 2:PP - win // 2], ALU.add))
                        own_wait(step)
                        s, h = dst[:, f:f + 2, PADP:], ph[:, f:f + 2, PADP:]
                        dve.scalar_tensor_tensor(out=pp[:, f:f + 2, PADP:], in0=s[:, :, PADP:], scalar=1.0 / win,
                                                 in1=h[:, :, PADP:], op0=ALU.mult, op1=ALU.subtract)
                        own_wait(own(dve.tensor_tensor(pp[:, f:f + 2, 0:PADP], s[:, :, 0:PADP],
                                                       share[:, lv:lv + 1, :].to_broadcast([P, 2, PADP]), ALU.mult)))
                        own_wait(own(dve.tensor_tensor(pp[:, f:f + 2, 0:PADP], pp[:, f:f + 2, 0:PADP], h[:, :, 0:PADP],
                                                       ALU.subtract)))
                        dve.tensor_copy(a_hi[:, f:f + 2, :], pp[:, f:f + 2, :]).then_inc(pp_ready, 1)
                        src, dst = dst, (pb if dst is pa else pa)
                    pieces(p + 4, p + 6)
                    for m in range(2):
                        dve.wait_ge(pool_done, m + 1)
                        for j in range(4):
                            f = 4 * m + j
                            ins = dve.tensor_scalar(tmp[:, f, :], job_banks(w + m)[:, j, :], col("pool_b_2", f),
                                                    col("pool_scale_2", f), ALU.add, ALU.mult)
                        ins.then_inc(bank_free[(w + m) % 2], 1)
                    post(g, w)
                elif st["kind"] == "ffn1":
                    def product(w, c, slot, n, i=0):
                        is_done(dve, c, i)
                        dve.wait_ge(sig_ready, n + 1)
                        dve.wait_ge(hid_ready, n + 1)
                        dve.tensor_tensor(ev[:, slot, :, :], sig[:, slot, :, :], job_banks(w)[:, 2:4, :], ALU.mult)\
                            .then_inc(bank_free[w % 2], 1)

                    n = st["hid"]

                    def two_jobs(i):
                        for b in range(2):
                            for u in range(2 * b, 2 * b + 2):
                                pieces(p + 4 + 2 * u, p + 6 + 2 * u, i)
                                mod_add(st["groups"][0], i, u)
                            product(w + b, c + 2 + 2 * b, b, n + 2 * i + b, i)

                    two_jobs(0)
                    with dve.Fori(1, 4) as i:
                        two_jobs(i)
                    for b in range(8, 11):
                        pieces(p + 4 * b + 4, p + 4 * b + 8)
                        product(w + b, c + 2 * b + 2, b % 2, n + b)
                    mod_finish(st["groups"][0], w + 12)
                    for m in range(2):
                        for u in range(8 * m, 8 * m + 8):
                            pieces(p + 48 + (3 * u + 1) // 2, p + 48 + (3 * u + 4) // 2)
                            mod_add(st["groups"][1], u // 4, u % 4)
                        residual(w + 11 + m, c + 28 + 6 * m, m, g)
                elif st["kind"] == "sb":
                    pieces(p + 4, p + 28)
                    for n in range(HEADS + 6):
                        if n < HEADS:
                            z = sb_z[:, n % 4, :]
                            dve.wait_ge(z_done, n + 1)
                            if n >= 4:
                                dve.wait_ge(e_ready, n - 3)
                            dve.tensor_scalar(z, bk[:, n % 2, 0:384], DH ** -0.5, None, ALU.mult).then_inc(z_copied, 1)
                            dve.wait_ge(z_copied, n + 1)
                            dve.scalar_tensor_tensor(out=sb_n[:, n % 4, :], in0=z, scalar=-1.0, in1=z,
                                                     op0=ALU.mult, op1=ALU.min).then_inc(n_ready, 1)
                        if 1 <= n <= HEADS:
                            h = n - 1
                            dve.wait_ge(l_ready, h + 1)
                            dve.scalar_tensor_tensor(out=sb_s[:, h % 4, :], in0=sb_z[:, h % 4, :], scalar=0.0,
                                                     in1=sb_l[:, h % 4, :], op0=ALU.max, op1=ALU.add)\
                                .then_inc(sp_ready, 1)
                        if 2 <= n < HEADS + 2:
                            h = n - 2
                            dve.wait_ge(suf_done, h + 1)
                            dve.tensor_tensor(sb_z[:, h % 4, :], sb_z[:, h % 4, :], bk[:, 2 + h % 2, 0:384],
                                              ALU.subtract).then_inc(t_ready, 1)
                        heads_out(n - 5)
                    for m in range(2):
                        pieces(p + 28 + 4 * m, p + 32 + 4 * m)
                        residual(w + 6 + m, c + 14 + 2 * m, m, g)
                elif st["kind"] == "lru":
                    pieces(p + 4, p + 24)
                    step = {}
                    for a in range(0, NB, 2):
                        for tap in range(1, TAPS):
                            for n in range(a, a + 2):
                                if tap == 1:
                                    dve.wait_ge(xc_first, n + 1)
                                else:
                                    own_wait(step[n])
                                ins = dve.scalar_tensor_tensor(out=lxc[:, n, :], in0=lxb[:, n, tap:tap + S],
                                                               scalar=col("lru_conv_w", 10 * tap + n), in1=lxc[:, n, :],
                                                               op0=ALU.mult, op1=ALU.add)
                                if tap < TAPS - 1:
                                    step[n] = own(ins)
                                else:
                                    ins.then_inc(xc_ready, 1)
                    for n in range(NB):
                        dve.wait_ge(a_ready, n + 1)
                        step[n] = own(dve.tensor_tensor(lri[:, n, 0, :], lxb[:, n, 0:S], lxb[:, n, 0:S], ALU.mult))
                    for n in range(NB):
                        own_wait(step[n])
                        dve.scalar_tensor_tensor(out=lri[:, n, 0, :], in0=lri[:, n, 0, :], scalar=1.0,
                                                 in1=lru_t(n), op0=ALU.add, op1=ALU.mult).then_inc(v_ready, 1)
                    for n in range(NB):
                        dve.wait_ge(s_ready, n + 1)
                        dve.wait_ge(ix_ready, n + 1)
                        step[n] = own(dve.tensor_tensor(lri[:, n, 1, :], lri[:, n, 0, :], lri[:, n, 1, :], ALU.mult))
                    for n in range(NB):
                        own_wait(step[n])
                        step[n] = own(dve.tensor_tensor_scan(lxc[:, n, :], lxb[:, n, 0:S], lri[:, n, 1, :], 0.0,
                                                             ALU.mult, ALU.add))
                    for n in range(NB):
                        own_wait(step[n])
                        step[n] = own(dve.tensor_tensor(lg[:, n, :], lg[:, n, :], lxc[:, n, :], ALU.mult))
                    for n in range(NB):
                        own_wait(step[n])
                        dve.tensor_copy(y_hi(n), lg[:, n, :]).then_inc(y_ready, 1)
                    for m in range(2):
                        pieces(p + 24 + 6 * m, p + 30 + 6 * m)
                        residual(w + 5 + m, c + 13 + 3 * m, m, g)

            if len(stages) <= 6:
                final_norm()
            for b in range(2):
                dve.wait_ge(turn_done, k.next("turn") + 1)
                ins = dve.tensor_copy(oout[:, b, :], job_flat(W_END + b, D))
            ins.then_inc(out_ready, 1)


_INS = ["x", "c", "mod_w", "mod_b", "norm_g", "ffn_w_gu", "ffn_w_down", "sb_w_qkv", "sb_w_o", "lru_w_in",
        "lru_conv_w", "lru_conv_b", "lru_w_r", "lru_b_r", "lru_w_i", "lru_b_i", "lru_lambda", "lru_w_out",
        "final_norm_g", "c_2", "positions_2", "ada_w_2", "ada_b_2", "norm_g_2", "mla_w_dq_2", "mla_q_norm_g_2",
        "mla_w_uq_2", "mla_w_dkv_2", "mla_kv_norm_g_2", "mla_w_ukv_2", "mla_w_o_2", "conv_w_pw1_2",
        "conv_b_pw1_2", "conv_w_dw_2", "conv_b_dw_2", "conv_ln_g_2", "conv_ln_b_2", "conv_w_pw2_2",
        "conv_b_pw2_2", "pool_w_2", "pool_b_2", "pool_scale_2", "ffn_w1_2", "ffn_w2_2"]


def kernel(**inputs):
    import concourse.bacc as bacc
    from concourse.bass_utils import run_bass_kernel_spmd

    nc = bacc.Bacc("TRN2", target_bir_lowering=False, num_devices=1)
    arrays, tensors = {}, {}
    for name in _INS:
        a = np.ascontiguousarray(inputs[name])
        arrays[f"in_{name}"] = a
        tensors[name] = nc.dram_tensor(f"in_{name}", a.shape, mybir.dt.from_np(a.dtype), kind="ExternalInput").ap()
    out = nc.dram_tensor("out", (1, S, D), F32, kind="ExternalOutput").ap()
    build(nc, tensors, out)
    got = run_bass_kernel_spmd(nc, [arrays], core_ids=[0])
    return got.results[0]["out"]
```

```python
from contextlib import ExitStack

import numpy as np

import concourse.bass as bass
from concourse import mybir

F32 = mybir.dt.float32
F32R = mybir.dt.float32r
I32 = mybir.dt.int32
ALU = mybir.AluOpType
ACT = mybir.ActivationFunctionType
AX_X = mybir.AxisListType.X

P = 128
D = 1024
S = 256
KD = D // P
F1 = 2816
F2 = 4096
DR = 1280
NB = DR // P
HEADS, DH = 16, 64
NOPE, ROPE, VH = 64, 32, 64
QL, KVL = 384, 256
TAPS, WIDTH = 4, 31
EPS = 1e-6
NEG = -1e30
WINDOWS = (2, 4, 8, 16)
PADP = WINDOWS[-1]
THETA = 10000.0
MODC = 3 * D

CH = 2048
PC = CH // 2
RAWS = 4
OPS = 4
MODW = MODC // 2
ARENA = 2 * F2 // P * S
FIRSTS = 7
UNITS = KD * MODC // MODW


def param_rows(shapes):
    at, n = {}, 0
    for name, count in shapes:
        at[name] = n
        n += count
    return at, n


class Counts:

    def __init__(self):
        self.n = {}

    def get(self, what):
        return self.n.get(what, 0)

    def add(self, what, by):
        self.n[what] = self.get(what) + by

    def next(self, what):
        self.add(what, 1)
        return self.get(what) - 1


def two_pi_parts():
    a = 6.28125
    b = float((np.float32(2 * np.pi - a).view(np.uint32) & np.uint32(0xFFFFF000)).view(np.float32))
    return a, b, float(2 * np.pi - a - b)


def tiles(pair, width=2):
    return bass.ds(pair * width, width)


def as_rows(a):
    names = "abcd"[:len(a.shape) - 1]
    return a.rearrange(f"{' '.join(names)} (n p) -> ({' '.join(names)} n) p", p=P)


def build(nc, t, out, stop=None):
    ctx = ExitStack()

    def sb(name, shape, dt=F32):
        return ctx.enter_context(nc.sbuf_tensor(name, shape, dt))

    def sem(name):
        return ctx.enter_context(nc.semaphore(name))

    with ctx:
        raw = sb("raw", [P, RAWS, CH])
        w_hi = sb("w_hi", [P, OPS, PC], F32R)
        w_lo = sb("w_lo", [P, OPS, PC], F32R)
        mod_raw = sb("mod_raw", [P, 2, MODW])
        mod_acc = sb("mod_acc", [P, MODC])
        x = sb("x", [P, KD, S])
        tmp = sb("tmp", [P, KD, S])
        a_hi = sb("a_hi", [P, KD, S], F32R)
        a_lo = sb("a_lo", [P, KD, S], F32R)
        sig = sb("sig", [P, 2, 2, S])
        ev = sb("ev", [P, 2, 2, S])
        ones = sb("ones", [P, P])
        one1 = sb("one1", [P, P])
        tri = sb("tri", [P, P])
        ident = sb("ident", [P, P])
        eps_col = sb("eps_col", [P, 1])
        lsp = sb("lsp", [P, 6, NB])
        rms = sb("rms", [P, 2, S])
        inv = sb("inv", [P, 2, S])
        rope = sb("rope", [P, S])
        rcol = sb("rcol", [P, 2])
        share = sb("share", [P, len(WINDOWS), PADP])
        top = sb("top", [P, HEADS, 2])
        low = sb("low", [P, HEADS, 2])
        total = sb("total", [P, HEADS, 2])
        part = sb("part", [P, HEADS, 2])
        cact = sb("cact", [P, 2 * KD])
        mv = sb("mv", [P, 14, 24])
        mv_a = sb("mv_a", [P, 14, KD])
        mv_g = sb("mv_g", [P, 14, KD])

        vec = [("mod_b", 2 * 72), ("norm_g", 48), ("final_norm_g", 8), ("c", 8),
               ("lru_conv_w", 40), ("lru_conv_b", 10), ("lru_b_r", 10), ("lru_b_i", 10), ("lru_lambda", 10),
               ("c_2", 8), ("ada_b_2", 4 * 48), ("norm_g_2", 4 * 4 * 8), ("mla_q_norm_g_2", 6),
               ("mla_kv_norm_g_2", 4), ("conv_b_pw1_2", 16), ("conv_w_dw_2", 8 * WIDTH), ("conv_b_dw_2", 8),
               ("conv_ln_g_2", 8), ("conv_ln_b_2", 8), ("conv_b_pw2_2", 8), ("pool_b_2", 8),
               ("pool_scale_2", 8)]
        ROW, NROW = param_rows(vec)
        vectors = {name: as_rows(t[name]) for name, _ in vec}
        for name, count in vec:
            assert vectors[name].shape[0] == count, (name, vectors[name].shape, count)
        NLOADS = 1 + sum((ROW[n] + m - 1) // P - ROW[n] // P + 1 for n, m in vec)
        NPT = -(-NROW // P)
        assert NPT <= 8
        cols = sb("cols", [P, NPT * P])

        def col(name, i, n=1):
            return cols[:, ROW[name] + i:ROW[name] + i + n]

        base = nc.sbuf_base
        arena = sb("arena", [P, ARENA])

        def place(layout):
            at, got = base, {}
            for name, shape, dt in layout:
                got[name] = nc.alloc_sbuf_tensor_at(name, shape, dt, offset=at)
                at += -(-4 * int(np.prod(shape[1:])) // 32) * 32
            assert at <= base + 4 * ARENA, (layout[0][0], at - base)
            return got

        v = place([("hid_hi", [P, 32, S], F32R), ("hid_lo", [P, 32, S], F32R)])
        hid_hi, hid_lo = v["hid_hi"], v["hid_lo"]
        v = place([("rows", [P, NPT, P], F32), ("xin", [P, 2, D], F32), ("rrow", [1, 2, P], F32),
                   ("first_mod", [P, FIRSTS, MODW], F32), ("pos_i", [1, S], I32), ("pos_f", [1, S], F32), ("turns_i", [P, S], I32)])
        first_mod = v["first_mod"]
        rows, xin, rrow, pos_i, pos_f, turns_i = (v[n] for n in ("rows", "xin", "rrow", "pos_i", "pos_f", "turns_i"))
        v = place([("qk", [P, 2 * KD, S], F32), ("vt", [P, 2, D], F32), ("sb_z", [P, 6, 384], F32),
                   ("sb_l", [P, 6, 384], F32), ("sb_s", [P, 6, 384], F32), ("sb_w", [P, 6, 384], F32)])
        qk, vt, sb_z, sb_l, sb_s, sb_w = (v[n] for n in ("qk", "vt", "sb_z", "sb_l", "sb_s", "sb_w"))

        def two(buf, m):
            return buf[:, 2 * (m % 3):2 * (m % 3) + 2, :]
        XP = S + TAPS - 1
        v = place([("lw", [P, 2 * NB, P], F32), ("lg", [P, NB, S], F32), ("lxb", [P, NB, XP], F32),
                   ("lxc", [P, NB, S], F32), ("lri", [P, NB, 2, S], F32)])
        lg, lxb, lxc, lw, lri = (v[n] for n in ("lg", "lxb", "lxc", "lw", "lri"))
        v = place([("more_hi", [P, NB - KD, S], F32R), ("more_lo", [P, NB - KD, S], F32R)])
        more_hi, more_lo = v["more_hi"], v["more_lo"]

        def y_hi(n):
            return a_hi[:, n, :] if n < KD else more_hi[:, n - KD, :]

        def y_lo(n):
            return a_lo[:, n, :] if n < KD else more_lo[:, n - KD, :]
        UP = S + WIDTH - 1
        CONV_DVE = 4
        DIAGS = 3
        v = place([("cu", [P, KD, UP], F32), ("cacc", [P, KD, S], F32), ("diag", [P, DIAGS, WIDTH, P], F32)])
        cu, cacc, diag = v["cu"], v["cacc"], v["diag"]
        PP = S + PADP
        v = place([("ph", [P, KD, PP], F32), ("pa", [P, KD, PP], F32), ("pb", [P, KD, PP], F32), ("pp", [P, KD, S], F32)])
        ph, pa, pb, pp = (v[n] for n in ("ph", "pa", "pb", "pp"))
        v = place([("qf", [P, HEADS, S], F32), ("kf", [P, HEADS, S], F32), ("mvt", [P, 2, D], F32),
                   ("cn", [P, 5, S], F32), ("cn_hi", [P, 5, S], F32R), ("cn_lo", [P, 5, S], F32R),
                   ("seen", [P, 384], F32)])
        qf, kf, mvt, cn, cn_hi, cn_lo, seen = (
            v[n] for n in ("qf", "kf", "mvt", "cn", "cn_hi", "cn_lo", "seen"))
        mp = place([("under_mp", [P, 2 * HEADS * S + 2 * D], F32), ("mp", [P, 6, 384], F32)])["mp"]
        mpt = tmp[:, 0:6, :].rearrange("p k s -> p (k s)").rearrange("p (n q) -> p n q", q=384)
        oout = place([("oout", [P, 2, D], F32)])["oout"]
        bk = ctx.enter_context(nc.psum_tensor("bk", [P, 8, 512], F32))

        landed = [sem(f"landed{i}") for i in range(RAWS)]
        hi_ready = sem("hi_ready")
        lo_ready = sem("lo_ready")
        piece_used = sem("piece_used")
        bank_free = [sem("bank_free0"), sem("bank_free1")]
        mod_landed = [sem(f"mod_landed{i}") for i in range(2)]
        first_landed = [sem(f"first_landed{i}") for i in range(FIRSTS)]
        mod_used = sem("mod_used")
        turn_done = sem("turn_done")
        turn_read = sem("turn_read")
        mod_ready = sem("mod_ready")
        sq_ready = sem("sq_ready")
        mean_done = sem("mean_done")
        rms_ready = sem("rms_ready")
        xn_ready = sem("xn_ready")
        h_ready = sem("h_ready")
        ahi_ready = sem("ahi_ready")
        act_ready = sem("act_ready")
        sig_ready = sem("sig_ready")
        hhi_ready = sem("hhi_ready")
        hid_ready = sem("hid_ready")
        z_done = sem("z_done")
        z_copied = sem("z_copied")
        n_ready = sem("n_ready")
        e1_ready = sem("e1_ready")
        l_ready = sem("l_ready")
        sp_ready = sem("sp_ready")
        spm_ready = sem("spm_ready")
        suf_done = sem("suf_done")
        t_ready = sem("t_ready")
        e_ready = sem("e_ready")
        w_ready = sem("w_ready")
        o_done = sem("o_done")
        ohi_ready = sem("ohi_ready")
        oact_ready = sem("oact_ready")
        lw_landed = sem("lw_landed")
        xb_zero = sem("xb_zero")
        xc_first = sem("xc_first")
        xc_ready = sem("xc_ready")
        ri_done = sem("ri_done")
        ri_ready = sem("ri_ready")
        ix_ready = sem("ix_ready")
        a_ready = sem("a_ready")
        v_ready = sem("v_ready")
        s_ready = sem("s_ready")
        y_ready = sem("y_ready")
        lact_ready = sem("lact_ready")
        x_done = sem("x_done")
        prod_ready = sem("prod_ready")
        pos_landed = sem("pos_landed")
        pool_landed = sem("pool_landed")
        pos_ready = sem("pos_ready")
        rope_read = sem("rope_read")
        rope_in = sem("rope_in")
        rope_arg = sem("rope_arg")
        rope_ready = sem("rope_ready")
        kv_done = sem("kv_done")
        ckv_out = sem("ckv_out")
        nope_out = sem("nope_out")
        cnh_ready = sem("cnh_ready")
        cn_ready = sem("cn_ready")
        qf_ready = sem("qf_ready")
        kr_ready = sem("kr_ready")
        seen_ready = sem("seen_ready")
        s_done = sem("s_done")
        sm_ready = sem("sm_ready")
        low_ready = sem("low_ready")
        p_ready = sem("p_ready")
        part_ready = sem("part_ready")
        pn_ready = sem("pn_ready")
        pt_done = sem("pt_done")
        pt_ready = sem("pt_ready")
        pool_done = sem("pool_done")
        cu_zero = sem("cu_zero")
        csig_ready = sem("csig_ready")
        conv_dve = sem("conv_dve")
        diag_ready = sem("diag_ready")
        dw_done = sem("dw_done")
        conv_act = sem("conv_act")
        xc2_ready = sem("xc2_ready")
        ph_zero = sem("ph_zero")
        pp_ready = sem("pp_ready")
        consts = sem("consts")
        loaded = sem("loaded")
        cact_ready = sem("cact_ready")
        dve_step = sem("dve_step")
        pool_step = sem("pool_step")
        out_ready = sem("out_ready")
        stored = sem("stored")

        kinds = ["ffn1", "sb", "ffn1", "ffn1", "lru", "ffn1", "mla", "ffn2", "conv", "ffn2", "pool", "ffn2", "mla", "ffn2"]
        CHUNKS = {"ffn1": 34, "sb": 16, "lru": 16, "mla": 14, "ffn2": 32, "conv": 12, "pool": 1}
        WJOBS = {"ffn1": 13, "sb": 8, "lru": 7, "mla": 12, "ffn2": 10, "conv": 7, "pool": 2}
        PAIRS = {"ffn1": 11, "ffn2": 16}
        GROUPS = {"ffn1": 2, "sb": 1, "mla": 1, "ffn2": 1}
        stages, c, w, hid, grp = [], 0, 0, 0, 1
        for n, kind in enumerate(kinds):
            groups = list(range(grp, min(grp + GROUPS.get(kind, 0), len(kinds))))
            late = stages[-1]["groups"][-1] if n and stages[-1]["groups"] else None
            stages.append(dict(kind=kind, n=n, c=c, w=w, hid=hid, groups=groups, late=late, nth=kinds[:n].count(kind)))
            c, w, hid, grp = c + CHUNKS[kind], w + WJOBS[kind], hid + PAIRS.get(kind, 0), grp + len(groups)
        if stop is not None:
            stages = stages[:stop]
        LAST_GROUP = max([0] + [h for z in stages for h in z["groups"]])
        st_pool = [z for z in stages if z["kind"] == "pool"]
        NPIECE = 2 * (stages[-1]["c"] + CHUNKS[stages[-1]["kind"]])
        act_base = [4 * (z["n"] + sum(y["kind"] == "conv" for y in stages[:z["n"]])) for z in stages]
        double = set()
        for st in stages:
            if st["kind"] == "ffn1":
                double |= {2 * (st["c"] + 27), 2 * (st["c"] + 33)}
            if st["kind"] == "lru":
                double |= {2 * (st["c"] + 12), 2 * (st["c"] + 15)}

        def split(p):
            h = p % 2
            whole = [(lambda o: o, lambda r: r[:, h * PC:h * PC + PC])]
            st = [z for z in stages if 2 * z["c"] <= p][-1]
            c = p // 2 - st["c"]
            if st["kind"] != "mla" or c >= 10:
                return whole
            if c >= 8:
                return [(lambda o, e=e: o[:, 512 * e:512 * e + 512].rearrange("p (h x) -> p h x", x=NOPE),
                         lambda r, e=e: r[:, h * PC:h * PC + PC].rearrange("p (h x) -> p h x", x=NOPE + VH)
                         [:, :, NOPE * e:NOPE * e + NOPE]) for e in range(2)]
            if c < 2:
                return [(lambda o: o[:, 0:2 * QL], lambda r: r[:, h * 2 * QL:(h + 1) * 2 * QL])]
            if c < 4:
                n, wide, at, cw = 2, KVL + ROPE, h * 2 * (KVL + ROPE), KVL + 2 * ROPE
                e = KVL
            else:
                n, wide, at, cw = (2 - h) * 4, NOPE + ROPE, h * 8 * (NOPE + ROPE), P
                e = NOPE
            o3 = lambda o: o[:, 0:n * cw].rearrange("p (a b) -> p a b", b=cw)
            r3 = lambda r: r[:, at:at + n * wide].rearrange("p (a b) -> p a b", b=wide)
            f = ROPE // 2
            return [(lambda o: o3(o)[:, :, 0:wide], lambda r: r3(r)),
                    (lambda o: o3(o)[:, :, wide:wide + f], lambda r: r3(r)[:, :, e + f:e + ROPE]),
                    (lambda o: o3(o)[:, :, wide + f:wide + ROPE], lambda r: r3(r)[:, :, e:e + f])]

        def sq_pair(q):
            return (sig, ev)[q // 2][:, q % 2, :, :]

        MEAN_CONV = sum({"mla": 4}.get(z["kind"], 1 + (z["n"] >= 6)) for z in stages[:8]) + 3
        W_END = w if stop is None else stages[-1]["w"] + WJOBS[stages[-1]["kind"]]

        def lru_t(n):
            return tmp[:, n, :] if n < KD else sig[:, 0, n - KD, :]

        def mod_of(g):
            return (t["mod_w"][g // 3], g % 3 * MODC) if g < 6 else (t["ada_w_2"][(g - 6) // 2], (g - 6) % 2 * MODC)

        def mod_bias(g):
            return col("mod_b", 24 * g, 24) if g < 6 else col("ada_b_2", 24 * (g - 6), 24)

        def is_free(eng, w, i=0):
            eng.wait_ge(bank_free[w % 2], w // 2 + 1 + i)

        def is_read(eng, w, i=0):
            eng.wait_ge(bank_free[w % 2], w // 2 + 2 + i)

        def is_done(eng, c, i=0):
            eng.wait_ge(piece_used, OPS + 2 * c + 8 * i)

        def job_banks(w, n=4, width=S):
            return bk[:, 4 * (w % 2):4 * (w % 2) + n, 0:width]

        def job_flat(w, n):
            return bk[:, 4 * (w % 2):4 * (w % 2) + 4, :].rearrange("p b n -> p (b n)")[:, 0:n]

        block = ctx.enter_context(nc.Block())

        @block.sync
        def _(sp):
            def chunk(c, src, view, i=0):
                sp.wait_ge(lo_ready, 2 * c + 2 + 8 * i)
                sp.dma_start(view(raw[:, c % RAWS, :]), src).then_inc(landed[c % RAWS], 16)

            def plain(c, w, kt, n, col0, i=0):
                chunk(c, w[kt * P:(kt + n) * P, :][:, bass.ds(col0, 512)].rearrange("(k p) m -> p k m", p=P),
                      lambda r: r[:, 0:n * 512].rearrange("p (k m) -> p k m", m=512), i)

            def some(c, w, kt, n, col0, wide):
                chunk(c, w[kt * P:(kt + n) * P, col0:col0 + wide].rearrange("(k p) m -> p k m", p=P),
                      lambda r: r[:, 0:n * wide].rearrange("p (k m) -> p k m", m=wide))

            def narrow(c, w, col0, i=0):
                chunk(c, w[:, bass.ds(col0, 256)].rearrange("(k p) m -> p k m", p=P),
                      lambda r: r.rearrange("p (k m) -> p k m", m=256), i)

            sp.dma_start(pos_i[:, :], t["positions_2"]).then_inc(pos_landed, 16)
            sp.dma_start(xin[:, :, :], t["x"][0].rearrange("(b p) d -> p b d", p=P)).then_inc(loaded, 16)
            for name, count in vec:
                src, r = vectors[name], 0
                while r < count:
                    a = ROW[name] + r
                    n = min(count - r, P - a % P)
                    sp.dma_start(rows[a % P:a % P + n, a // P, :], src[r:r + n, :]).then_inc(loaded, 16)
                    r += n
            for u in range(UNITS):
                if u >= FIRSTS:
                    sp.wait_ge(mod_used, 2 + u - FIRSTS + 1)
                w, at = mod_of(0)
                sp.dma_start(first_mod[:, u % FIRSTS, :], w[u // 2 * P:u // 2 * P + P, at + u % 2 * MODW:at + (u % 2 + 1) * MODW])\
                    .then_inc(first_landed[u % FIRSTS], 16)

            for st in stages:
                c = st["c"]
                if st["kind"] == "ffn1":
                    wg, wd = t["ffn_w_gu"][st["n"] // 3, st["n"] % 3 // 2], t["ffn_w_down"][st["n"] // 3, st["n"] % 3 // 2]
                    with sp.Fori(0, 5) as i:
                        for b in range(4):
                            narrow(c + b, wg, (2 * i + b // 2) * 256 + b % 2 * F1, i)
                    for b in range(2):
                        narrow(c + 20 + b, wg, 10 * 256 + b * F1)
                    for m in range(2):
                        for k in range(6):
                            plain(c + 22 + 6 * m + k, wd, 4 * k, min(4, 22 - 4 * k), 512 * m)
                elif st["kind"] == "sb":
                    with sp.Fori(0, 3) as i:
                        for b in range(4):
                            plain(c + b, t["sb_w_qkv"][0], 4 * (b % 2), 4, (2 * i + b // 2) * 512, i)
                    for b in range(4):
                        plain(c + 12 + b, t["sb_w_o"][0], 4 * (b % 2), 4, 512 * (b // 2))
                elif st["kind"] == "lru":
                    is_done(sp, c)
                    for g, name in enumerate(("lru_w_r", "lru_w_i")):
                        sp.dma_start(lw[:, g * NB:(g + 1) * NB, :], t[name][0].rearrange("n k j -> k n j"))\
                          .then_inc(lw_landed, 16)
                    with sp.Fori(0, 2) as i:
                        for b in range(4):
                            plain(c + b, t["lru_w_in"][0], 4 * (b % 2), 4, (2 * i + b // 2) * 512, i)
                    for b in range(2):
                        plain(c + 8 + b, t["lru_w_in"][0], 4 * b, 4, 2048)
                    for m in range(2):
                        for k in range(3):
                            plain(c + 10 + 3 * m + k, t["lru_w_out"][0], 4 * k, min(4, 10 - 4 * k), 512 * m)
                elif st["kind"] == "ffn2":
                    w1, w2 = t["ffn_w1_2"][st["nth"]], t["ffn_w2_2"][st["nth"]]
                    with sp.Fori(0, 4) as i:
                        for b in range(4):
                            narrow(c + b, w1, (4 * i + b) * 256, i)
                    for m in range(2):
                        for k in range(8):
                            plain(c + 16 + 8 * m + k, w2, 4 * k, 4, 512 * m)
                elif st["kind"] == "mla":
                    n = st["nth"]
                    for b in range(2):
                        some(c + b, t["mla_w_dq_2"][n], 4 * b, 4, 0, QL)
                    for b in range(2):
                        some(c + 2 + b, t["mla_w_dkv_2"][n], 4 * b, 4, 0, KVL + ROPE)
                    for b in range(4):
                        some(c + 4 + b, t["mla_w_uq_2"][n], 0, QL // P, b * 384, 384)
                    for b in range(2):
                        some(c + 8 + b, t["mla_w_ukv_2"][n], 0, KVL // P, b * 1024, 1024)
                    for b in range(4):
                        plain(c + 10 + b, t["mla_w_o_2"][n], 4 * (b % 2), 4, 512 * (b // 2))
                elif st["kind"] == "conv":
                    for b in range(8):
                        narrow(c + b, t["conv_w_pw1_2"][0], b // 2 * 256 + (1 - b % 2) * D)
                    for b in range(4):
                        plain(c + 8 + b, t["conv_w_pw2_2"][0], 4 * (b % 2), 4, 512 * (b // 2))
                elif st["kind"] == "pool":
                    sp.wait_ge(lo_ready, 2 * c + 2)
                    for kt in range(2):
                        sp.dma_start(raw[:, c % RAWS, kt * PC:(kt + 1) * PC].rearrange("p (g m) -> p g m", m=256),
                                     t["pool_w_2"][0].rearrange("g (k p) m -> k p g m", p=P)[kt])\
                            .then_inc(landed[c % RAWS] if kt else pool_landed, 16)
            sp.wait_ge(out_ready, 1)
            sp.dma_start(out[0].rearrange("(b p) d -> p b d", p=P), oout[:, :, :]).then_inc(stored, 16)
            sp.wait_ge(stored, 16)

        @block.gpsimd
        def _(pool):
            k = Counts()

            def mod_half(g, r, h):
                w, at = mod_of(g)
                pool.wait_ge(mod_used, UNITS * g + 2 * r + h + 1)
                pool.dma_start(mod_raw[:, h, :].unsqueeze(1),
                               w.rearrange("(k p) m -> p k m", p=P)[:, bass.ds(r, 1),
                                   at + h * MODW:at + (h + 1) * MODW]).then_inc(mod_landed[h], 16)

            def mod_load(g, r):
                for h in range(2):
                    mod_half(g, r, h)

            def mod_unit(g, u):
                if u < UNITS:
                    mod_half(g, u // 2, u % 2)
                elif g < LAST_GROUP:
                    mod_half(g + 1, 0, u - UNITS)

            def mod_next(g, r):
                if r < KD:
                    mod_load(g, r)
                elif g < LAST_GROUP:
                    mod_load(g + 1, 0)

            def mod_rest(g, beside=None):
                with pool.Fori(0, 3) as i:
                    for b in range(2):
                        mod_load(g, 2 * i + b + 1)
                        if beside is not None:
                            beside(i, b)
                for b in range(2):
                    mod_next(g, 7 + b)
                    if beside is not None:
                        beside(3, b)

            def act_low():
                for q in range(4):
                    pool.wait_ge(ahi_ready, k.next("ahi") + 1)
                    pool.tensor_tensor(a_lo[:, 2 * q:2 * q + 2, :], tmp[:, 2 * q:2 * q + 2, :],
                                       a_hi[:, 2 * q:2 * q + 2, :].bitcast(F32), ALU.subtract).then_inc(act_ready, 1)

            def hid_low(n, pair, slot, width=2):
                pool.wait_ge(hhi_ready, n + 1)
                pool.tensor_tensor(hid_lo[:, tiles(pair, width), :], ev[:, slot, :, :],
                                   hid_hi[:, tiles(pair, width), :].bitcast(F32), ALU.subtract).then_inc(hid_ready, 1)

            def keep_earlier(buf, ready, m, done):
                pool.wait_ge(ready, m + 1)
                for e in range(2):
                    own_keys = two(buf, m)[:, e, :].rearrange("p (b q) -> p b q", q=P)[:, 0:3:2, :]
                    ins = pool.affine_select(out=own_keys, in_=own_keys, compare_op=ALU.is_gt, fill=0.0, base=0,
                                             pattern=[[0, 2], [1, P]], channel_multiplier=-1)
                ins.then_inc(done, 1)

            pool.memset(eps_col[:, :], EPS)
            pool.memset(ident[:, :], 0.0).then_inc(pool_step, 1)
            pool.wait_ge(pool_step, 1)
            pool.affine_select(out=ident[:, :], in_=ident[:, :], compare_op=ALU.not_equal, fill=1.0, base=0,
                               pattern=[[-1, P]], channel_multiplier=1).then_inc(consts, 1)
            pool.memset(ones[:, :], 1.0 / D).then_inc(consts, 1)
            pool.memset(one1[:, :], 1.0).then_inc(consts, 1)
            for g, win in enumerate(WINDOWS):
                pool.memset(share[:, g, :], 1.0 / win)
            freqs = np.power(np.float32(THETA), -np.arange(0, ROPE, 2, dtype=np.float32) / np.float32(ROPE))
            pool.memset(rrow[:, 0, 0:NOPE], 0.0)
            for f in range(ROPE // 2):
                pool.memset(rrow[:, 0, NOPE + f:P:ROPE // 2], float(freqs[f]))
            pool.memset(rrow[:, 1, :], 1.0).then_inc(pool_step, 1)
            pool.wait_ge(pool_step, 2)
            pool.memset(rrow[:, 1, 96:112], -1.0)
            for g, win in enumerate(WINDOWS):
                for s in range(win):
                    pool.memset(share[:, g, s:s + 1], 1.0 / (s + 1))
            pool.wait_ge(consts, 3)
            pool.affine_select(out=tri[:, :], in_=one1[:, :], compare_op=ALU.is_ge, fill=0.0, base=0,
                               pattern=[[-1, P]], channel_multiplier=1).then_inc(consts, 1)
            if LAST_GROUP:
                mod_load(1, 0)

            def heads_low():
                for m in range(HEADS // 2):
                    if st["groups"] and m:
                        mod_next(st["groups"][0], m)
                    pool.wait_ge(part_ready, k.next("part") + 1)
                    for e in range(2):
                        for a in range(2):
                            b = two(mp, m)[:, e, P * a:P + 2 * P * a]
                            ins = pool.tensor_scalar(b, b, part[:, 2 * m + e, a:a + 1], None, ALU.mult)
                    ins.then_inc(pn_ready, 1)
                if st["groups"]:
                    mod_next(st["groups"][0], KD)

            for st in stages:
                if st["kind"] != "pool":
                    act_low()
                if st["kind"] == "ffn2":
                    g, n = st["groups"], st["hid"]

                    def two_low(i, b):
                        for e in range(2):
                            hid_low(n + 4 * i + 2 * b + e, 4 * i + 2 * b + e, e)

                    with pool.Fori(0, 4) as i:
                        for b in range(2):
                            two_low(i, b)
                            if g and b == 1:
                                mod_load(g[0], i + 1)
                    if g:
                        for r in range(5, KD + 1):
                            mod_next(g[0], r)
                elif st["kind"] == "mla":
                    pool.memset(seen[:, :], 0.0).then_inc(pool_step, 1)
                    pool.wait_ge(pool_step, 3 + k.next("pstep"))
                    pool.memset(seen[0:64, 64:P], NEG)
                    pool.memset(seen[0:64, 320:384], NEG).then_inc(seen_ready, 1)
                    for a, b in ((0, 2), (2, 3), (3, 5)):
                        pool.wait_ge(cnh_ready, k.next("cn") + 1)
                        pool.tensor_tensor(cn_lo[:, a:b, :], cn[:, a:b, :], cn_hi[:, a:b, :].bitcast(F32), ALU.subtract)\
                            .then_inc(cn_ready, 1)
                    heads_low()
                elif st["kind"] == "conv":
                    pool.memset(cu[:, :, 0:WIDTH - 1], 0.0).then_inc(cu_zero, 1)
                    for n in range(CONV_DVE, KD):
                        if n - CONV_DVE >= DIAGS:
                            pool.wait_ge(dw_done, n - CONV_DVE - DIAGS + 1)
                        for tap in range(WIDTH):
                            ins = pool.tensor_scalar(diag[:, (n - CONV_DVE) % DIAGS, tap, :], ident[:, :],
                                                     col("conv_w_dw_2", KD * tap + n), None, ALU.mult)
                        ins.then_inc(diag_ready, 1)
                    act_low()
                elif st["kind"] == "pool":
                    for buf in (ph, pa, pb):
                        ins = pool.memset(buf[:, :, 0:PADP], 0.0)
                    ins.then_inc(ph_zero, 1)
                    for q in range(4):
                        pool.wait_ge(pp_ready, q + 1)
                        pool.tensor_tensor(a_lo[:, 2 * q:2 * q + 2, :], pp[:, 2 * q:2 * q + 2, :],
                                           a_hi[:, 2 * q:2 * q + 2, :].bitcast(F32), ALU.subtract).then_inc(act_ready, 1)
                elif st["kind"] == "ffn1":
                    g, n = st["groups"][0], st["hid"]
                    mod_rest(g, lambda i, b: hid_low(n + 2 * i + b, 2 * i + b, b))
                    for b in range(3):
                        if b:
                            mod_next(g + 1, b)
                        hid_low(n + 8 + b, 8 + b, b % 2)
                    for r in range(3, KD + 1):
                        mod_next(g + 1, r)
                elif st["kind"] == "sb":
                    for m in range(HEADS // 2 + 2):
                        if 2 <= m <= KD:
                            mod_next(st["groups"][0], m - 1)
                        if 1 <= m <= HEADS // 2:
                            keep_earlier(sb_s, sp_ready, m - 1, spm_ready)
                        if m >= 2:
                            keep_earlier(sb_w, e_ready, m - 2, w_ready)
                    mod_next(st["groups"][0], KD)
                elif st["kind"] == "lru":
                    pool.memset(lxb[:, :, 0:TAPS - 1], 0.0).then_inc(xb_zero, 1)
                    for n in range(NB):
                        pool.wait_ge(ri_ready, n + 1)
                        pool.tensor_tensor(lri[:, n, 1, :], lri[:, n, 1, :], lxc[:, n, :], ALU.mult)\
                            .then_inc(ix_ready, 1)
                    for n in range(NB):
                        pool.wait_ge(y_ready, n + 1)
                        pool.tensor_tensor(y_lo(n), lg[:, n, :], y_hi(n).bitcast(F32),
                                           ALU.subtract).then_inc(lact_ready, 1)

        @block.scalar
        def _(act):
            k = Counts()
            act.sem_inc(bank_free[0], 1)
            act.sem_inc(bank_free[1], 1)

            def pieces(a, b, i=0):
                for p in range(a, b):
                    c = p // 2
                    if p >= NPIECE or p - 1 in double:
                        continue
                    act.wait_ge(piece_used, p + 1 + 8 * i)
                    act.wait_ge(landed[c % RAWS], 16 * (c // RAWS + 1) + 16 * i)
                    if st_pool and p == 2 * st_pool[0]["c"]:
                        act.wait_ge(pool_landed, 16)
                    for o, r in split(p):
                        ins = act.activation(o(w_hi[:, p % OPS, :]), r(raw[:, c % RAWS, :]), ACT.Copy)
                    ins.then_inc(hi_ready, 2 if p in double else 1)

            def squares(src, dst, n):
                for q in range(0, n, 2):
                    act.activation(dst[:, q:min(q + 2, n), :], src[:, q:min(q + 2, n), :], ACT.Square)\
                        .then_inc(sq_ready, 1)

            def x_squares(w):
                for m in range(2):
                    if k.get("normed") == 0 and w:
                        is_read(act, w - 2 + m)
                    for q in range(2 * m, 2 * m + 2):
                        if k.get("normed"):
                            act.wait_ge(x_done, k.next("xd") + 1)
                        squares(x[:, 2 * q:2 * q + 2, :], tmp[:, 2 * q:2 * q + 2, :], 2)

            def root(w, scale=1.0):
                act.wait_ge(mean_done, k.next("mean") + 1)
                act.activation(rms[:, k.next("root") % 2, :], job_flat(w, S), ACT.Sqrt, bias=eps_col[:, 0:1], scale=scale).then_inc(rms_ready, 1)

            def modulate(func, scale, bias, out=None):
                for q in range(4):
                    act.wait_ge(xn_ready, k.next("xn") + 1)
                    for j in range(2 * q, 2 * q + 2):
                        ins = act.activation((out or (lambda j: tmp[:, j, :]))(j), tmp[:, j, :], func,
                                             bias=bias(j), scale=scale(j))
                    ins.then_inc(h_ready, 1)

            def final_norm(w):
                x_squares(w)
                root(w)
                k.add("normed", 1)

            def post_squares(w):
                for m in range(2):
                    is_read(act, w + m)
                    for q in range(2 * m, 2 * m + 2):
                        squares(tmp[:, 2 * q:2 * q + 2, :], sq_pair(q), 2)

            def y_out(w, m, bias=None):
                y = tmp[:, 4 * m:4 * m + 4, :]
                if bias is None:
                    act.activation(y, job_banks(w + m), ACT.Copy).then_inc(bank_free[(w + m) % 2], 1)
                    return
                for j in range(4):
                    ins = act.activation(y[:, j, :], job_banks(w + m)[:, j, :], ACT.Identity, bias=col(bias, 4 * m + j))
                ins.then_inc(bank_free[(w + m) % 2], 1)

            def heads_out(n):
                if n >= 0 and n % 2 == 0 and n // 2 < HEADS // 2:
                    act.wait_ge(o_done, k.next("o") + 1)
                    act.activation(a_hi[:, n // 2, :], bk[:, 4 + n // 2 % 2, 0:S], ACT.Copy).then_inc(ohi_ready, 1)

            act.wait_ge(consts, 1)
            act.wait_ge(turn_read, 2)
            act.activation(cact[:, 0:KD], col("c", 0, KD), ACT.Silu)
            act.activation(cact[:, KD:2 * KD], col("c_2", 0, KD), ACT.Silu)
            act.activation(lsp[:, 0, :], col("lru_lambda", 0, NB), ACT.Abs).then_inc(cact_ready, 1)
            act.wait_ge(cact_ready, 1)
            act.activation(lsp[:, 1, :], lsp[:, 0, :], ACT.Exp, scale=-1.0).then_inc(cact_ready, 1)
            pieces(0, 2)

            for st in stages:
                p, c, w, g = 2 * st["c"], st["c"], st["w"], st["n"]
                if g == 6:
                    final_norm(w)
                x_squares(w)
                pieces(p + 2, p + 4)
                root(w)
                if g == 0:
                    act.wait_ge(rope_arg, 1)
                    act.activation(rope[NOPE:P, :], ev[NOPE:P, 0, 0, :], ACT.Sin).then_inc(rope_ready, 1)
                act.wait_ge(mod_ready, g + 1)
                if st["kind"] == "pool":
                    act.wait_ge(ph_zero, 1)
                modulate(ACT.Identity, lambda j: mv_a[:, g, j:j + 1], lambda j: mv[:, g, j:j + 1],
                         (lambda j: ph[:, j, PADP:]) if st["kind"] == "pool" else None)
                if st["kind"] == "ffn2":
                    def relu(w, c, i, e):
                        is_done(act, c + 1 + e, i)
                        act.activation(sig[:, e, :, :], job_banks(w)[:, 2 * e:2 * e + 2, :], ACT.Relu).then_inc(sig_ready, 1)

                    with act.Fori(0, 4) as i:
                        for b in range(2):
                            pieces(p + 4 + 4 * b, p + 8 + 4 * b, i)
                            for e in range(2):
                                relu(w + b, c + 2 * b, i, e)
                            for e in range(2):
                                if e:
                                    is_read(act, w + b, i)
                                else:
                                    act.wait_ge(prod_ready, 8 * st["nth"] + 2 * i + b + 1)
                                act.activation(hid_hi[:, tiles(4 * i + 2 * b + e), :], ev[:, e, :, :], ACT.Copy)\
                                    .then_inc(hhi_ready, 1)
                    for m in range(2):
                        pieces(p + 36 + 16 * m, p + 52 + 14 * m)
                        is_done(act, c + 24 + 8 * m)
                        y_out(w + 8, m)
                    post_squares(w + 8)
                    root(w + 10)
                elif st["kind"] == "mla":
                    pieces(p + 4, p + 8)
                    is_done(act, c + 2)
                    act.activation(cn[:, 0:3, :], job_banks(w, 3), ACT.Copy).then_inc(bank_free[w % 2], 1)
                    is_read(act, w)
                    squares(cn[:, 0:2, :], sq_pair(0), 2)
                    squares(cn[:, 2:3, :], sq_pair(1)[:, 0:1, :], 1)
                    pieces(p + 8, p + 12)
                    is_done(act, c + 4)
                    act.activation(cn[:, 3:5, :], job_banks(w + 1, 2), ACT.Copy).then_inc(ckv_out, 1)
                    act.wait_ge(ckv_out, st["nth"] + 1)
                    squares(cn[:, 3:5, :], sq_pair(2), 2)
                    root(w + 2, D / QL)
                    root(w + 3, D / KVL)
                    for b in range(4):
                        pieces(p + 12 + 2 * b, p + 14 + 2 * b)
                        is_done(act, c + 5 + b)
                        act.activation(qf[0:NOPE, 4 * b:4 * b + 4, :], job_banks(w + 2 + b)[0:NOPE], ACT.Copy)\
                            .then_inc(nope_out, 1)
                    for b in range(2):
                        kv_job = w + 6 + 2 * b
                        act.wait_ge(kv_done, 4 * st["nth"] + 2 * b + 1)
                        for e in range(2):
                            ins = act.activation(kf[0:NOPE, 8 * b + e:8 * b + 8:2, :],
                                                 job_banks(kv_job)[NOPE * e:NOPE * e + NOPE], ACT.Copy)
                        ins.then_inc(bank_free[kv_job % 2], 1)
                        act.wait_ge(kv_done, 4 * st["nth"] + 2 * b + 2)
                        act.activation(mvt[:, :, 512 * b:512 * b + 512], job_banks(kv_job + 1, 2, 512), ACT.Copy)\
                            .then_inc(bank_free[(kv_job + 1) % 2], 1)
                        pieces(p + 20 + 2 * b, p + 22 + 2 * b)
                    scale = (NOPE + ROPE) ** -0.5
                    o0 = k.get("o")
                    act.wait_ge(qf_ready, 4 * st["nth"] + 4)
                    m0 = HEADS // 2 * st["nth"]
                    for m in range(HEADS // 2 + 4):
                        if m < HEADS // 2:
                            act.wait_ge(low_ready, m0 + m + 1)
                            for n in (2 * m, 2 * m + 1):
                                for a in range(2):
                                    s = two(mp, m)[:, n % 2, P * a:P + 2 * P * a]
                                    ins = act.activation(s, s, ACT.Exp, bias=low[:, n, a:a + 1], scale=scale,
                                                         accum_out=total[:, n, a:a + 1])
                            ins.then_inc(p_ready, 1)
                        if 2 <= m < HEADS // 2 + 2:
                            h = m - 2
                            act.wait_ge(pt_done, m0 + h + 1)
                            if h >= 2:
                                act.wait_ge(o_done, o0 + h - 1)
                            act.activation(mpt[:, 2 * (h % 2):2 * (h % 2) + 2, :], bk[:, 2:4, 0:384], ACT.Copy)\
                                .then_inc(pt_ready, 1)
                        heads_out(2 * (m - 4))
                    pieces(p + 24, p + 28)
                    for m in range(2):
                        pieces(p + 28 + 2 * m, p + 30)
                        is_done(act, c + 12 + 2 * m)
                        y_out(w + 10, m)
                    post_squares(w + 10)
                    root(w + 12)
                elif st["kind"] == "conv":
                    with act.Fori(0, 2) as i:
                        for b in range(2):
                            pieces(p + 4 + 4 * b, p + 8 + 4 * b, i)
                            is_done(act, c + 1 + 2 * b, i)
                            for e in range(2):
                                ins = act.activation(sig[:, b, e, :], job_banks(w + b)[:, e, :], ACT.Sigmoid,
                                                     bias=cols[:, bass.ds(4 * i + ROW["conv_b_pw1_2"] + KD + 2 * b + e, 1)])
                            ins.then_inc(csig_ready, 1)
                    for n in range(CONV_DVE, KD):
                        act.wait_ge(dw_done, n - CONV_DVE + 1)
                        act.activation(cacc[:, n, :], job_banks(w + 4)[:, n - CONV_DVE, :], ACT.Identity,
                                       bias=col("conv_b_dw_2", n)).then_inc(conv_act, 1)
                    act.wait_ge(conv_act, KD - CONV_DVE)
                    act.sem_inc(bank_free[w % 2], 1)
                    for q in range(4):
                        act.wait_ge(xc2_ready, q + 1)
                        squares(tmp[:, 2 * q:2 * q + 2, :], sq_pair(q), 2)
                    k.add("mean", 1)
                    root(w + 6)
                    modulate(ACT.Silu, lambda j: col("conv_ln_g_2", j), lambda j: col("conv_ln_b_2", j))
                    for m in range(2):
                        pieces(p + 20 + 4 * m, p + 24 + 2 * m)
                        is_done(act, c + 10 + 2 * m)
                        y_out(w + 5, m, "conv_b_pw2_2")
                    post_squares(w + 5)
                    root(w + 7)
                elif st["kind"] == "pool":
                    post_squares(w)
                    root(w + 2)
                elif st["kind"] == "ffn1":
                    n = st["hid"]

                    def gated(w, slot, pair, i=0):
                        act.activation(sig[:, slot, :, :], job_banks(w, 2), ACT.Silu).then_inc(sig_ready, 1)
                        is_read(act, w, i)
                        act.activation(hid_hi[:, tiles(pair, 2), :], ev[:, slot, :, :], ACT.Copy)\
                            .then_inc(hhi_ready, 1)

                    with act.Fori(0, 4) as i:
                        for b in range(2):
                            pieces(p + 4 + 4 * b, p + 8 + 4 * b, i)
                            is_done(act, c + 1 + 2 * b, i)
                            gated(w + b, b, 2 * i + b, i)
                    for b in range(8, 11):
                        pieces(p + 4 * b + 4, p + 4 * b + 8)
                        is_done(act, c + 2 * b + 1)
                        gated(w + b, b % 2, b)
                    pieces(p + 48, p + 70)
                elif st["kind"] == "sb":
                    with act.Fori(0, 2) as i:
                        for b in range(2):
                            pieces(p + 4 + 4 * b, p + 8 + 4 * b, i)
                            is_done(act, c + 2 + 2 * b, i)
                            act.activation(qk[:, bass.ds(8 * i + 4 * b, 4), :], job_banks(w + b), ACT.Copy)\
                                .then_inc(bank_free[(w + b) % 2], 1)
                    for b in range(2):
                        pieces(p + 20 + 4 * b, p + 24 + 4 * b)
                        is_done(act, c + 10 + 2 * b)
                        act.activation(vt[:, :, 512 * b:512 * b + 512], job_banks(w + 4 + b, 2, 512), ACT.Copy)\
                            .then_inc(bank_free[(w + b) % 2], 1)
                    for m in range(HEADS // 2 + 4):
                        if m < HEADS // 2:
                            act.wait_ge(n_ready, m + 1)
                            act.activation(two(sb_l, m), two(sb_l, m), ACT.Exp).then_inc(e1_ready, 1)
                        if 2 <= m < HEADS // 2 + 2:
                            act.wait_ge(t_ready, m - 1)
                            act.activation(two(sb_w, m - 2), two(sb_z, m - 2), ACT.Exp).then_inc(e_ready, 1)
                        if m < HEADS // 2:
                            act.wait_ge(e1_ready, m + 1)
                            act.activation(two(sb_l, m), two(sb_l, m), ACT.Ln, bias=1.0).then_inc(l_ready, 1)
                        heads_out(2 * (m - 4))
                    pieces(p + 28, p + 34)
                elif st["kind"] == "lru":
                    for b in range(5):
                        pieces(p + 4 + 4 * b, p + 8 + 4 * b)
                        is_done(act, c + 2 + 2 * b)
                        first = 4 * b
                        for a, e, f in ((first, min(first + 4, NB), 0), (max(first, NB), first + 4, 1)):
                            if a >= e:
                                continue
                            bks = job_banks(w + b)[:, a - first:e - first, :]
                            if f:
                                ins = act.activation(lxb[:, a - NB:e - NB, TAPS - 1:], bks, ACT.Copy)
                            else:
                                ins = act.activation(lg[:, a:e, :], bks, ACT.Gelu_apprx_tanh)
                        ins.then_inc(bank_free[(w + b) % 2], 1)
                        for n in range(max(first - NB, 0), first + 4 - NB):
                            if n == 0:
                                act.wait_ge(xb_zero, 1)
                            is_read(act, w + b)
                            act.activation(lxc[:, n, :], lxb[:, n, 0:S], ACT.Identity,
                                           bias=col("lru_conv_b", n), scale=col("lru_conv_w", n)).then_inc(xc_first, 1)
                    for n in range(NB):
                        act.wait_ge(ri_done, n + 1)
                        act.activation(lri[:, n, 0, :], bk[:, n % 8, 0:S], ACT.Sigmoid, bias=col("lru_b_r", n))
                        act.activation(lri[:, n, 1, :], bk[:, n % 8, S:2 * S], ACT.Sigmoid, bias=col("lru_b_i", n))\
                            .then_inc(ri_ready, 1)
                    for n in range(NB):
                        act.wait_ge(ri_ready, n + 1)
                        act.activation(lxb[:, n, 0:S], lri[:, n, 0, :], ACT.Exp, scale=lsp[:, 4, n:n + 1])
                        act.activation(lru_t(n), lri[:, n, 0, :], ACT.Tanh, scale=lsp[:, 5, n:n + 1])\
                            .then_inc(a_ready, 1)
                    for n in range(NB):
                        act.wait_ge(v_ready, n + 1)
                        act.activation(lri[:, n, 0, :], lri[:, n, 0, :], ACT.Sqrt).then_inc(s_ready, 1)
                    pieces(p + 24, p + 34)

            if len(stages) <= 6:
                final_norm(W_END)

        @block.tensor
        def _(pe):
            k = Counts()
            pe.sem_inc(piece_used, OPS)

            def piece(p, i, ready, xs, kt, outs, first, last):
                if ready is not None:
                    pe.wait_ge(*ready)
                pe.wait_ge(lo_ready, 2 * RAWS + p + 1 + 8 * i)
                n = 2
                for r in range(n):
                    wh, wl = (z[:, p % OPS, 512 * r:512 * r + 512] for z in (w_hi, w_lo))
                    xh, xl = (z(kt + r) for z in xs)
                    f, l = first and r == 0, last and r == n - 1
                    ins = outs(wh, wl, xh, xl, f, l)
                ins.then_inc(piece_used, 2 if p in double else 1)

            def by_feature(w):
                def go(wh, wl, xh, xl, first, last):
                    for m in range(4):
                        o = job_banks(w)[:, m, :]
                        s = slice(P * m, P * m + P)
                        pe.matmul(o, wh[:, s], xh, start=first, stop=False)
                        pe.matmul(o, wh[:, s], xl, start=False, stop=False)
                        ins = pe.matmul(o, wl[:, s], xh, start=False, stop=last)
                    return ins
                return go

            def by_token(w):
                def go(wh, wl, xh, xl, first, last):
                    for b in range(2):
                        o = job_banks(w, 2, 512)[:, b, :]
                        s = slice(P * b, P * b + P)
                        pe.matmul(o, xh[:, s], wh, start=first, stop=False)
                        pe.matmul(o, xh[:, s], wl, start=False, stop=False)
                        ins = pe.matmul(o, xl[:, s], wh, start=False, stop=last)
                    return ins
                return go

            def job(c, w, i, xs, kt0, kts, ready, outs=None):
                is_free(pe, w, i)
                n = (kts + 1) // 2
                for q in range(n):
                    piece(2 * c + q, i, ready(q) if ready else None, xs, kt0 + 2 * q, outs or by_feature(w),
                          q == 0, q == n - 1)

            def gate_up(c, w, i, act_from=None, second=None):
                is_free(pe, w, i)
                for q in range(4):
                    p = 2 * c + q
                    pe.wait_ge(lo_ready, 2 * RAWS + p + 1 + 8 * i)
                    for r in range(4):
                        f = q % 2 * 4 + r
                        if act_from is not None and q < 2 and f % 2 == 0:
                            pe.wait_ge(act_ready, act_from + f // 2 + 1)
                        for m in range(2):
                            o = job_banks(w)[:, q // 2 * 2 + m, :]
                            wh, wl = (z[:, p % OPS, 256 * r + P * m:256 * r + P * m + P] for z in (w_hi, w_lo))
                            pe.matmul(o, wh, a_hi[:, f, :], start=(f == 0), stop=False)
                            pe.matmul(o, wh, a_lo[:, f, :], start=False, stop=False)
                            ins = pe.matmul(o, wl, a_hi[:, f, :], start=False, stop=(f == KD - 1))
                    ins.then_inc(piece_used, 1)
                    if second is not None and q == 1:
                        second()

            def mean(w, src, n, ready=None):
                is_free(pe, w)
                for j in range(n):
                    if ready is not None:
                        ready(j)
                    elif j % 2 == 0:
                        pe.wait_ge(sq_ready, k.next("sq") + 1)
                    ins = pe.matmul(job_flat(w, S), ones[:, :], src(j), start=(j == 0), stop=(j == n - 1))
                ins.then_inc(mean_done, 1)
                k.add("root", 1)

            def y_mean(w):
                mean(w, lambda j: sq_pair(j // 2)[:, j % 2, :], KD)

            def x_mean(w):
                mean(w, lambda j: tmp[:, j, :], KD)

            def head_out(h, v, wt, ready):
                m, r = h // 2, slice(DH * (h % 2), DH * (h % 2) + DH)
                pe.wait_ge(*ready)
                if h % 2 == 0 and m >= 2:
                    pe.wait_ge(oact_ready, k.get("oact") + m - 1)
                o = bk[r, 4 + m % 2, :]
                pe.matmul(o[:, 0:S], v[:, 0, DH * h:DH * h + DH], wt[:, 0:S], start=True, stop=False)
                ins = pe.matmul(o[:, P:S], v[:, 1, DH * h:DH * h + DH], wt[:, S:384], start=False, stop=True)
                if h % 2:
                    ins.then_inc(o_done, 1)
                if h == HEADS - 1:
                    k.add("oact", HEADS // 2)

            def turn(w, blocks):
                is_free(pe, w)
                for j, b in enumerate(blocks):
                    r = b.shape[0]
                    ins = pe.transpose(job_flat(w, 2048)[:, P * j:P * j + r], b, ident[0:r, 0:r])
                ins.then_inc(turn_done, 1)
                k.add("turn", 1)

            def mod_sum(g, w, a=0, b=MODC // P):
                if a == 0:
                    is_free(pe, w)
                    pe.wait_ge(mod_used, 2 + UNITS * (g + 1))
                for j in range(a, b):
                    ins = pe.matmul(job_banks(w)[:, 1, j:j + 1], mod_acc[:, P * j:P * j + P], one1[:, 0:1],
                                    start=True, stop=True)
                if b == MODC // P:
                    ins.then_inc(turn_done, 1)
                    k.add("turn", 1)

            def turned():
                pe.wait_ge(turn_read, k.get("turn"))

            pe.wait_ge(consts, 1)
            pe.wait_ge(loaded, 16 * NLOADS)
            turn(0, [xin[:, b, P * j:P * j + P] for j in range(KD) for b in range(2)])
            turn(1, [rows[0:min(P, NROW - P * j), j, :] for j in range(NPT)])
            turned()
            pe.wait_ge(pos_ready, 1)
            pe.wait_ge(consts, 4)
            for j in range(2):
                pe.matmul(bk[:, 0, j:j + 1], rrow[:, j, :], one1[0:1, 0:1], start=True, stop=True)
            pe.matmul(bk[:, 1, 0:S], one1[0:1, :], pos_f[:, :], start=True, stop=True).then_inc(rope_in, 1)
            mod_sum(0, 1)
            turned()
            pe.wait_ge(rope_read, 1)

            for st in stages:
                c, w, g = st["c"], st["w"], st["n"]
                A = (y_hi, y_lo)
                H = (lambda f: hid_hi[:, f, :], lambda f: hid_lo[:, f, :])
                if g == 6:
                    x_mean(w)
                if st["late"]:
                    mod_sum(st["late"], w, 0, 8)
                x_mean(w)
                if st["late"]:
                    mod_sum(st["late"], w, 8)
                    turned()
                nq = act_base[g]
                act_in = lambda q: (act_ready, nq + q + 1)
                if st["kind"] == "ffn2":
                    with pe.Fori(0, 4) as i:
                        for b in range(2):
                            gate_up(c + 2 * b, w + b, i, nq)
                    for m in range(2):
                        job(c + 16 + 8 * m, w + 8 + m, 0, H, 0, F2 // P,
                            (lambda q: (hid_ready, 2 + st["hid"] + q + 1)) if m == 0 else None)
                    y_mean(w + 10)
                elif st["kind"] == "mla":
                    C = (lambda f: cn_hi[:, f, :], lambda f: cn_lo[:, f, :])
                    nc_ = 3 * st["nth"]

                    def by_columns(w, starts):
                        def go(p, r, f, xs, first, last):
                            wh, wl = (z[:, p % OPS, :] for z in (w_hi, w_lo))
                            xh, xl = (z(f) for z in xs)
                            for m, a in enumerate(starts(r)):
                                o = job_banks(w)[:, m, :]
                                pe.matmul(o, wh[:, a:a + P], xh, start=first, stop=False)
                                pe.matmul(o, wh[:, a:a + P], xl, start=False, stop=False)
                                ins = pe.matmul(o, wl[:, a:a + P], xh, start=False, stop=last)
                            return ins
                        return go

                    for n, (width, starts) in enumerate(((QL, (0, P, 2 * P)), (KVL + 2 * ROPE, (0, P, KVL - NOPE)))):
                        is_free(pe, w + n)
                        go = by_columns(w + n, lambda r: [r * width + a for a in starts])
                        for q in range(4):
                            p = 2 * (c + 2 * n) + q
                            if n == 0:
                                pe.wait_ge(*act_in(q))
                            pe.wait_ge(lo_ready, 2 * RAWS + p + 1)
                            for r in range(2):
                                ins = go(p, r, 2 * q + r, A, q == 0 and r == 0, q == 3 and r == 1)
                            ins.then_inc(piece_used, 1)
                    mean(w + 2, lambda j: sq_pair(j // 2)[:, j % 2, :], 3)
                    mean(w + 3, lambda j: sq_pair(2)[:, j, :], 2)
                    for b in range(4):
                        is_free(pe, w + 2 + b)
                        if b == 1:
                            pe.wait_ge(rms_ready, k.get("root"))
                        go = by_columns(w + 2 + b, lambda r: [r * 512 + P * m for m in range(4)])
                        for q in range(2):
                            p = 2 * (c + 4 + b) + q
                            if b == 0:
                                pe.wait_ge(cn_ready, nc_ + q + 1)
                            pe.wait_ge(lo_ready, 2 * RAWS + p + 1)
                            for r in range(2 - q):
                                ins = go(p, r, 2 * q + r, C, q == 0 and r == 0, q == 1)
                            ins.then_inc(piece_used, 1)
                    pe.wait_ge(cn_ready, nc_ + 3)
                    for b in range(2):
                        p = 2 * (c + 8 + b)
                        j = w + 6 + 2 * b
                        is_free(pe, j)
                        for r in range(2):
                            pe.wait_ge(lo_ready, 2 * RAWS + p + r + 1)
                            wh, wl = (z[:, (p + r) % OPS, :] for z in (w_hi, w_lo))
                            xh, xl = (z(3 + r) for z in C)
                            for m in range(4):
                                o, s = job_banks(j)[:, m, :], slice(P * m, P * m + P)
                                pe.matmul(o, wh[:, s], xh, start=(r == 0), stop=False)
                                pe.matmul(o, wh[:, s], xl, start=False, stop=False)
                                ins = pe.matmul(o, wl[:, s], xh, start=False, stop=(r == 1))
                        ins.then_inc(kv_done, 1)
                        is_free(pe, j + 1)
                        for a in range(2):
                            for r in range(2):
                                wh, wl = (z[:, (p + r) % OPS, 512:] for z in (w_hi, w_lo))
                                xh, xl = (z(3 + r)[:, P * a:P * a + P] for z in C)
                                o = job_banks(j + 1, 2, 512)[:, a, :]
                                pe.matmul(o, xh, wh, start=(r == 0), stop=False)
                                pe.matmul(o, xh, wl, start=False, stop=False)
                                ins = pe.matmul(o, xl, wh, start=False, stop=(r == 1))
                        ins.then_inc(kv_done, 1)
                        pe.wait_ge(kv_done, 4 * st["nth"] + 2 * b + 2)
                        pe.sem_inc(piece_used, 2)
                    for j in (w + 8, w + 9):
                        is_read(pe, j)
                    pe.wait_ge(qf_ready, 4 * st["nth"] + 4)
                    pe.wait_ge(kr_ready, st["nth"] + 1)
                    m0 = HEADS // 2 * st["nth"]
                    for m in range(HEADS // 2 + 3):
                        if m < HEADS // 2:
                            if m >= 2:
                                pe.wait_ge(sm_ready, m0 + m - 1)
                            r = slice(0, NOPE + ROPE)
                            for e in range(2):
                                n, o = 2 * m + e, bk[:, 6 * (m % 2) + e, :]
                                pe.matmul(o[:, 0:P], qf[r, n, 0:P], kf[r, n, 0:P], start=True, stop=True)
                                ins = pe.matmul(o[:, P:384], qf[r, n, P:S], kf[r, n, :], start=True, stop=True)
                            ins.then_inc(s_done, 1)
                        if 2 <= m < HEADS // 2 + 2:
                            h = m - 2
                            pe.wait_ge(pn_ready, m0 + h + 1)
                            if h >= 1:
                                pe.wait_ge(pt_ready, m0 + h)
                            for e in range(2):
                                for a in range(3):
                                    ins = pe.transpose(bk[:, 2 + e, P * a:P * a + P],
                                                       two(mp, h)[:, e, P * a:P * a + P], ident[:, :])
                            ins.then_inc(pt_done, 1)
                        if m >= 3:
                            h = m - 3
                            for e in range(2):
                                head_out(2 * h + e, mvt, mpt[:, 2 * (h % 2) + e, :], (pt_ready, m0 + h + 1))
                    pe.wait_ge(oact_ready, k.get("oact"))
                    for m in range(2):
                        job(c + 10 + 2 * m, w + 10 + m, 0, A, 0, KD, None)
                    y_mean(w + 12)
                elif st["kind"] == "conv":
                    with pe.Fori(0, 2) as i:
                        for b in range(2):
                            gate_up(c + 2 * b, w + b, i, nq)

                    def convolved(j):
                        if j < CONV_DVE:
                            pe.wait_ge(conv_dve, j + 1)
                        else:
                            pe.wait_ge(conv_act, j - CONV_DVE + 1)
                    is_free(pe, w + 4)
                    for n in range(CONV_DVE, KD):
                        if n % 2 == 0 or n == CONV_DVE:
                            is_read(pe, w + n // 2)
                        pe.wait_ge(diag_ready, n - CONV_DVE + 1)
                        for tap in range(WIDTH):
                            ins = pe.matmul(job_banks(w + 4)[:, n - CONV_DVE, :], diag[:, (n - CONV_DVE) % DIAGS, tap, :],
                                            cu[:, n, tap:tap + S], start=(tap == 0), stop=(tap == WIDTH - 1))
                        ins.then_inc(dw_done, 1)
                    mean(w + 5, lambda j: cacc[:, j, :], KD, convolved)
                    k.add("root", -1)
                    y_mean(w + 6)
                    for m in range(2):
                        job(c + 8 + 2 * m, w + 5 + m, 0, A, 0, KD, (lambda q: (act_ready, nq + 4 + q + 1)) if m == 0 else None)
                    y_mean(w + 7)
                elif st["kind"] == "pool":
                    for m in range(2):
                        is_free(pe, w + m)
                        for r in range(2):
                            pe.wait_ge(lo_ready, 2 * RAWS + 2 * c + r + 1)
                            wh, wl = (z[:, (2 * c + r) % OPS, :] for z in (w_hi, w_lo))
                            for e in range(4):
                                g_ = 2 * m + e // 2
                                if m == 0 and r == 0 or e % 2 == 0:
                                    pe.wait_ge(act_ready, nq + g_ + 1)
                                o, s = job_banks(w + m)[:, e, :], slice(256 * g_ + P * (e % 2), 256 * g_ + P * (e % 2) + P)
                                xh, xl = a_hi[:, 2 * g_ + r, :], a_lo[:, 2 * g_ + r, :]
                                pe.matmul(o, wh[:, s], xh, start=(r == 0), stop=False)
                                pe.matmul(o, wh[:, s], xl, start=False, stop=False)
                                ins = pe.matmul(o, wl[:, s], xh, start=False, stop=(r == 1))
                        ins.then_inc(pool_done, 1)
                    pe.wait_ge(pool_done, 2)
                    pe.sem_inc(piece_used, 2)
                    y_mean(w + 2)
                elif st["kind"] == "ffn1":
                    with pe.Fori(0, 4) as i:
                        for b in range(2):
                            gate_up(c + 2 * b, w + b, i, nq)
                    for b in range(8, 11):
                        gate_up(c + 2 * b, w + b, 0, second=(lambda: mod_sum(st["groups"][0], w + 9)) if b == 8 else None)
                        turned()
                    for m in range(2):
                        job(c + 22 + 6 * m, w + 11 + m, 0, H, 0, 22,
                            (lambda q: (hid_ready, 2 + st["hid"] + q + 1)) if m == 0 else None)
                elif st["kind"] == "sb":
                    with pe.Fori(0, 2) as i:
                        for b in range(2):
                            job(c + 2 * b, w + b, i, A, 0, KD, act_in)
                    for b in range(2):
                        job(c + 8 + 2 * b, w + 4 + b, 0, A, 0, KD, None, by_token(w + 4 + b))
                    is_read(pe, w + 4)
                    is_read(pe, w + 5)
                    for m in range(HEADS // 2 + 3):
                        if m < HEADS // 2:
                            if m >= 2:
                                pe.wait_ge(z_copied, m - 1)
                            for e in range(2):
                                r, o = slice(DH * e, DH * e + DH), bk[:, 6 * (m % 2) + e, :]
                                pe.matmul(o[:, 0:S], qk[r, KD + m, 0:P], qk[r, m, :], start=True, stop=True)
                                ins = pe.matmul(o[:, S:384], qk[r, KD + m, P:S], qk[r, m, P:S], start=True, stop=True)
                            ins.then_inc(z_done, 1)
                        if 1 <= m <= HEADS // 2:
                            pe.wait_ge(spm_ready, m)
                            if m >= 2:
                                pe.wait_ge(t_ready, m - 1)
                            for e in range(2):
                                o, s = bk[:, 2 + e, :], two(sb_s, m - 1)[:, e, :]
                                pe.matmul(o[:, 0:S], tri[:, :], s[:, 0:S], start=True, stop=False)
                                pe.matmul(o[:, P:S], one1[:, :], s[:, S:384], start=False, stop=True)
                                ins = pe.matmul(o[:, S:384], tri[:, :], s[:, S:384], start=True, stop=True)
                            ins.then_inc(suf_done, 1)
                        if m >= 3:
                            for e in range(2):
                                head_out(2 * (m - 3) + e, vt, two(sb_w, m - 3)[:, e, :], (w_ready, m - 2))
                    pe.wait_ge(oact_ready, HEADS // 2)
                    for m in range(2):
                        job(c + 12 + 2 * m, w + 6 + m, 0, A, 0, KD, None)
                elif st["kind"] == "lru":
                    for b in range(5):
                        job(c + 2 * b, w + b, 0, A, 0, KD, act_in if b == 0 else None)
                    is_read(pe, w + 3)
                    is_read(pe, w + 4)
                    pe.wait_ge(lw_landed, 32)
                    for n in range(NB):
                        pe.wait_ge(xc_ready, n + 1)
                        if n >= 8:
                            pe.wait_ge(ri_ready, n - 7)
                        pe.matmul(bk[:, n % 8, 0:S], lw[:, n, :], lxc[:, n, :], start=True, stop=True)
                        pe.matmul(bk[:, n % 8, S:2 * S], lw[:, NB + n, :], lxc[:, n, :], start=True, stop=True)\
                            .then_inc(ri_done, 1)
                    pe.wait_ge(ri_ready, NB)
                    for m in range(2):
                        job(c + 10 + 3 * m, w + 5 + m, 0, A, 0, NB,
                            (lambda q: (lact_ready, 2 * q + 2)) if m == 0 else None)
            if len(stages) <= 6:
                x_mean(W_END)
            pe.wait_ge(x_done, 4 + 4 * max(0, len(stages) - 6))
            for b in range(2):
                is_free(pe, W_END + b)
                for j in range(KD):
                    ins = pe.transpose(job_flat(W_END + b, D)[:, P * j:P * j + P], x[:, j, P * b:P * b + P], ident[:, :])
                ins.then_inc(turn_done, 1)

        @block.vector
        def _(dve):
            k = Counts()
            dve.sem_inc(lo_ready, 2 * RAWS)
            dve.sem_inc(mod_used, 2)
            dve.sem_inc(hid_ready, 2)

            def own(ins):
                ins.then_inc(dve_step, 1)
                return k.next("step") + 1

            def own_wait(n):
                dve.wait_ge(dve_step, n)

            def pieces(a, b, i=0):
                for p in range(a, b):
                    c = p // 2
                    if p >= NPIECE or p - 1 in double:
                        continue
                    dve.wait_ge(hi_ready, p + 1 + 8 * i)
                    for o, r in split(p):
                        ins = dve.tensor_tensor(o(w_lo[:, p % OPS, :]), r(raw[:, c % RAWS, :]),
                                                o(w_hi[:, p % OPS, :].bitcast(F32)), ALU.subtract)
                    ins.then_inc(lo_ready, 2 if p in double else 1)

            def mod_add(g, r, h):
                cc = cact[:, 0:KD] if g < 6 else cact[:, KD:2 * KD]
                if g == 0:
                    u = 2 * r + h
                    src = first_mod[:, u % FIRSTS, :]
                    dve.wait_ge(first_landed[u % FIRSTS], 16 * (u // FIRSTS + 1))
                else:
                    src = mod_raw[:, h, :]
                    dve.wait_ge(mod_landed[h], 16 * (UNITS // 2 * (g - 1) + r + 1))
                dve.wait_ge(mod_used, UNITS * g + 2 * r + h + 1)
                a = mod_acc[:, h * MODW:(h + 1) * MODW]
                if isinstance(r, int) and r == 0:
                    dve.tensor_scalar(a, src, cc[:, 0:1], None, ALU.mult).then_inc(mod_used, 1)
                    return
                dve.scalar_tensor_tensor(out=a, in0=src, scalar=cc[:, bass.ds(r, 1)],
                                         in1=a, op0=ALU.mult, op1=ALU.add).then_inc(mod_used, 1)

            def turn_in(dst, w, n):
                dve.wait_ge(turn_done, k.next("turn") + 1)
                dve.tensor_copy(dst, job_flat(w, n)).then_inc(turn_read, 1)

            def mod_finish(g, w):
                dve.wait_ge(turn_done, k.next("turn") + 1)
                dve.tensor_tensor(mv[:, g, :], job_banks(w)[:, 1, 0:MODC // P], mod_bias(g), ALU.add).then_inc(turn_read, 1)
                dve.wait_ge(turn_read, k.get("turn"))
                gain = col("norm_g", 8 * g, 8) if g < 6 else col("norm_g_2", 16 * (g - 6), 8)
                dve.scalar_tensor_tensor(out=mv_a[:, g, :], in0=mv[:, g, 8:16], scalar=1.0, in1=gain,
                                         op0=ALU.add, op1=ALU.mult)
                gate = mv[:, g, 16:24]
                if g >= 6:
                    ins = dve.tensor_tensor(mv_g[:, g, :], gate, col("norm_g_2", 16 * (g - 6) + 8, 8), ALU.mult)
                elif g % 3 == 1:
                    ins = dve.tensor_scalar(mv_g[:, g, :], gate, 1.0, None, ALU.add)
                else:
                    ins = dve.tensor_scalar(mv_g[:, g, :], gate, 1.0, 0.5, ALU.add, ALU.mult)
                ins.then_inc(mod_ready, 1)

            def inverse():
                s = k.get("rms") % 2
                dve.wait_ge(rms_ready, k.next("rms") + 1)
                own_wait(own(dve.reciprocal(inv[:, s, :], rms[:, s, :])))
                return inv[:, s, :]

            def normed(src, dst, n, ready, iv):
                for q in range(0, n, 2):
                    e = min(q + 2, n)
                    dve.tensor_tensor(dst[:, q:e, :], src[:, q:e, :], iv.unsqueeze(1).to_broadcast([P, e - q, S]),
                                      ALU.mult).then_inc(ready, 1)

            def final_norm():
                iv = inverse()
                for j in range(KD):
                    ins = dve.scalar_tensor_tensor(out=x[:, j, :], in0=x[:, j, :], scalar=col("final_norm_g", j),
                                                   in1=iv, op0=ALU.mult, op1=ALU.mult)
                    if j % 2:
                        ins.then_inc(x_done, 1)

            def post(g, w):
                iv = inverse()
                step = [own(dve.tensor_tensor(tmp[:, 2 * q:2 * q + 2, :], tmp[:, 2 * q:2 * q + 2, :],
                                              iv.unsqueeze(1).to_broadcast([P, 2, S]), ALU.mult)) for q in range(4)]
                for j in range(KD):
                    if j % 2 == 0:
                        own_wait(step[j // 2])
                    ins = dve.scalar_tensor_tensor(out=x[:, j, :], in0=tmp[:, j, :], scalar=mv_g[:, g, j:j + 1],
                                                   in1=x[:, j, :], op0=ALU.mult, op1=ALU.add)
                    if j % 2:
                        ins.then_inc(x_done, 1)

            def heads_out(n):
                if n >= 0 and n % 2 == 0 and n // 2 < HEADS // 2:
                    m = n // 2
                    dve.wait_ge(ohi_ready, k.next("ohi") + 1)
                    dve.tensor_tensor(a_lo[:, m, :], bk[:, 4 + m % 2, 0:S], a_hi[:, m, :].bitcast(F32),
                                      ALU.subtract).then_inc(oact_ready, 1)

            def act_high():
                for q in range(4):
                    dve.wait_ge(h_ready, k.next("h") + 1)
                    dve.tensor_copy(a_hi[:, 2 * q:2 * q + 2, :], tmp[:, 2 * q:2 * q + 2, :]).then_inc(ahi_ready, 1)

            def residual(w, c, m, g):
                is_done(dve, c)
                for j in range(4):
                    f = 4 * m + j
                    ins = dve.scalar_tensor_tensor(out=x[:, f, :], in0=job_banks(w)[:, j, :],
                                                   scalar=mv_g[:, g, f:f + 1], in1=x[:, f, :],
                                                   op0=ALU.mult, op1=ALU.add)
                ins.then_inc(bank_free[w % 2], 1)

            dve.wait_ge(pos_landed, 16)
            dve.tensor_copy(pos_f[:, :], pos_i[:, :]).then_inc(pos_ready, 1)
            turn_in(x[:, :, :].rearrange("p k s -> p (k s)"), 0, 2048)
            turn_in(cols[:, 0:NROW], 1, NROW)
            dve.wait_ge(turn_read, 2)
            dve.wait_ge(cact_ready, 2)
            for r in range(KD):
                for h in range(2):
                    mod_add(0, r, h)
            u, r, r2, s = (lsp[:, j, :] for j in (1, 2, 3, 0))
            own_wait(own(dve.tensor_scalar(r, u, 2.0, None, ALU.add)))
            own_wait(own(dve.reciprocal(r2, r)))
            own_wait(own(dve.tensor_tensor(r, u, r2, ALU.mult)))
            own_wait(own(dve.tensor_tensor(r2, r, r, ALU.mult)))
            own_wait(own(dve.tensor_scalar(s, r2, 1.0 / 17, 1.0 / 15, ALU.mult, ALU.add)))
            for d in (13, 11, 9, 7, 5, 3, 1):
                own_wait(own(dve.tensor_tensor(s, s, r2, ALU.mult)))
                own_wait(own(dve.tensor_scalar(s, s, 1.0 / d, None, ALU.add)))
            own_wait(own(dve.scalar_tensor_tensor(out=s, in0=s, scalar=2.0, in1=r, op0=ALU.mult, op1=ALU.mult)))
            own_wait(own(dve.tensor_scalar(r, col("lru_lambda", 0, NB), -1.0, 0.0, ALU.mult, ALU.max)))
            own_wait(own(dve.tensor_tensor(s, s, r, ALU.add)))
            dve.tensor_scalar(lsp[:, 4, :], s, -8.0, None, ALU.mult)
            dve.tensor_scalar(lsp[:, 5, :], s, 8.0, None, ALU.mult)
            dve.wait_ge(rope_in, 1)
            own_wait(own(dve.tensor_copy(rcol[:, :], bk[:, 0, 0:2])))
            ang, tr, red = ev[:, 0, 0, :], ev[:, 0, 1, :], ev[:, 1, 0, :]
            dve.tensor_scalar(ang, bk[:, 1, 0:S], rcol[:, 0:1], None, ALU.mult).then_inc(rope_read, 1)
            dve.wait_ge(rope_read, 1)
            own_wait(own(dve.tensor_scalar(turns_i[:, :], ang, 1.0 / (2 * np.pi), None, ALU.mult)))
            own_wait(own(dve.tensor_copy(tr, turns_i[:, :])))
            parts = two_pi_parts()
            for n, cst in enumerate(parts):
                own_wait(own(dve.scalar_tensor_tensor(out=red if n % 2 == 0 else ang, in0=tr, scalar=-cst,
                                                      in1=ang if n % 2 == 0 else red, op0=ALU.mult, op1=ALU.add)))
            own_wait(own(dve.tensor_scalar(ang, red, 3.1415925, -3.1415925, ALU.min, ALU.max)))
            own_wait(own(dve.tensor_scalar(red, ang, -1.0, None, ALU.mult)))
            own_wait(own(dve.tensor_tensor(tr, ang, red, ALU.min)))
            own_wait(own(dve.tensor_scalar(red, ang, rcol[:, 1:2], None, ALU.mult)))
            dve.tensor_copy(ev[NOPE + ROPE:P, 0, 0, :], ev[NOPE + ROPE:P, 1, 0, :])
            dve.tensor_scalar(ev[NOPE:NOPE + ROPE, 0, 0, :], ev[NOPE:NOPE + ROPE, 0, 1, :], float(np.pi / 2), None, ALU.add)\
                .then_inc(rope_arg, 1)

            mod_finish(0, 1)
            pieces(0, 2)

            for st in stages:
                p, c, w, g = 2 * st["c"], st["c"], st["w"], st["n"]
                if g == 6:
                    final_norm()
                pieces(p + 2, p + 4)
                normed(x, tmp, KD, xn_ready, inverse())
                if st["kind"] != "pool":
                    act_high()
                if st["late"]:
                    mod_finish(st["late"], w)
                if st["kind"] == "ffn2":
                    n = st["hid"]

                    def two_jobs(i):
                        for b in range(2):
                            pieces(p + 4 + 4 * b, p + 8 + 4 * b, i)
                            if st["groups"]:
                                mod_add(st["groups"][0], i, b)
                            for e in range(2):
                                dve.wait_ge(sig_ready, n + 2 * b + e + 1 + 4 * i)
                                dve.wait_ge(hid_ready, n + 2 * b + e + 1 + 4 * i)
                                dve.tensor_tensor(ev[:, e, :, :], sig[:, e, :, :], sig[:, e, :, :], ALU.mult)\
                                    .then_inc(bank_free[(w + b) % 2] if e else prod_ready, 1)

                    two_jobs(0)
                    with dve.Fori(1, 4) as i:
                        two_jobs(i)
                    for u in range(8):
                        pieces(p + 36 + 4 * u, p + 39 + 4 * u - u // 7)
                        if st["groups"]:
                            mod_add(st["groups"][0], 4 + u // 2, u % 2)
                        if u < 7:
                            pieces(p + 39 + 4 * u, p + 40 + 4 * u)
                    post(g, w + 8)
                elif st["kind"] == "mla":
                    pieces(p + 4, p + 12)
                    def rotate(src, a, b, last):
                        n = src.shape[1]
                        tab = lambda r: rope[r, :].unsqueeze(1).to_broadcast([ROPE, n, S])
                        C_, S_ = slice(NOPE, NOPE + ROPE), slice(NOPE + ROPE, P)
                        own(dve.tensor_tensor(a, src[C_], tab(C_), ALU.mult))
                        dve.tensor_tensor(b, src[S_], tab(S_), ALU.mult).then_inc(*last)

                    dve.wait_ge(ckv_out, st["nth"] + 1)
                    dve.wait_ge(rope_ready, 1)
                    R = slice(NOPE, NOPE + ROPE)
                    a, b_, kr = ev[R, 1, 0:1, :], ev[R, 1, 1:2, :], sig[R, 1, 1:2, :]
                    rotate(job_banks(w + 1)[:, 2:3, :], a, b_, (bank_free[(w + 1) % 2], 1))
                    own_wait(k.get("step"))
                    is_read(dve, w + 1)
                    own_wait(own(dve.tensor_tensor(kr, a, b_, ALU.add)))
                    dve.tensor_copy(kf[R, :, :], kr.to_broadcast([ROPE, HEADS, S])).then_inc(kr_ready, 1)
                    for a0, name, first, count in (("q", "mla_q_norm_g_2", 0, 3), ("kv", "mla_kv_norm_g_2", 3, 2)):
                        iv = inverse()
                        step = []
                        for j in range(count):
                            step.append(own(dve.scalar_tensor_tensor(
                                out=cn[:, first + j, :], in0=cn[:, first + j, :], scalar=col(name, count * st["nth"] + j),
                                in1=iv, op0=ALU.mult, op1=ALU.mult)))
                        own_wait(step[-1])
                        for j in range(0, count, 2):
                            e = min(j + 2, count)
                            dve.tensor_copy(cn_hi[:, first + j:first + e, :], cn[:, first + j:first + e, :])\
                                .then_inc(cnh_ready, 1)
                    for b in range(4):
                        pieces(p + 12 + 2 * b, p + 14 + 2 * b)
                        dve.wait_ge(nope_out, 4 * st["nth"] + b + 1)
                        if b:
                            dve.wait_ge(qf_ready, 4 * st["nth"] + b)
                        rotate(job_banks(w + 2 + b), tmp[R, 0:4, :], tmp[R, 4:8, :], (bank_free[(w + b) % 2], 1))
                        own_wait(k.get("step"))
                        is_read(dve, w + 2 + b)
                        dve.tensor_tensor(qf[R, 4 * b:4 * b + 4, :], tmp[R, 0:4, :], tmp[R, 4:8, :], ALU.add)\
                            .then_inc(qf_ready, 1)
                    pieces(p + 20, p + 24)
                    dve.wait_ge(seen_ready, st["nth"] + 1)
                    m0 = HEADS // 2 * st["nth"]
                    for m in range(HEADS // 2 + 4):
                        if m < HEADS // 2:
                            dve.wait_ge(s_done, m0 + m + 1)
                            if m >= 3:
                                dve.wait_ge(pt_done, m0 + m - 2)
                            dve.tensor_tensor(two(mp, m), bk[:, 6 * (m % 2):6 * (m % 2) + 2, 0:384],
                                              seen[:, :].unsqueeze(1).to_broadcast([P, 2, 384]), ALU.add)\
                                .then_inc(sm_ready, 1)
                            dve.wait_ge(sm_ready, m0 + m + 1)
                            for a in range(2):
                                ins = dve.tensor_reduce(top[:, 2 * m:2 * m + 2, a:a + 1],
                                                        two(mp, m)[:, :, P * a:P + 2 * P * a], AX_X, ALU.max)
                            own_wait(own(ins))
                            dve.tensor_scalar(low[:, 2 * m:2 * m + 2, :], top[:, 2 * m:2 * m + 2, :],
                                              -(NOPE + ROPE) ** -0.5, None, ALU.mult).then_inc(low_ready, 1)
                        if 1 <= m <= HEADS // 2:
                            dve.wait_ge(p_ready, m0 + m)
                            dve.reciprocal(part[:, 2 * m - 2:2 * m, :], total[:, 2 * m - 2:2 * m, :])\
                                .then_inc(part_ready, 1)
                            if st["groups"]:
                                for h in range(2):
                                    mod_add(st["groups"][0], m - 1, h)
                        heads_out(2 * (m - 4))
                    pieces(p + 24, p + 30)
                    post(g, w + 10)
                elif st["kind"] == "conv":
                    dve.wait_ge(cu_zero, 1)
                    with dve.Fori(0, 2) as i:
                        for b in range(2):
                            pieces(p + 4 + 4 * b, p + 8 + 4 * b, i)
                            is_done(dve, c + 2 + 2 * b, i)
                            dve.wait_ge(csig_ready, b + 1 + 2 * i)
                            for e in range(2):
                                ins = dve.scalar_tensor_tensor(
                                    out=cu[:, bass.ds(4 * i + 2 * b + e, 1), WIDTH - 1:],
                                    in0=job_banks(w + b)[:, 2 + e:3 + e, :],
                                    scalar=cols[:, bass.ds(4 * i + ROW["conv_b_pw1_2"] + 2 * b + e, 1)],
                                    in1=sig[:, b, e:e + 1, :], op0=ALU.add, op1=ALU.mult)
                            ins.then_inc(bank_free[(w + b) % 2], 1)
                    step = {}
                    for tap in range(WIDTH):
                        for n in range(CONV_DVE):
                            if tap == 0:
                                if n % 2 == 0:
                                    is_read(dve, w + n // 2)
                                ins = dve.tensor_scalar(cacc[:, n, :], cu[:, n, 0:S], col("conv_w_dw_2", n),
                                                        col("conv_b_dw_2", n), ALU.mult, ALU.add)
                            else:
                                own_wait(step[n])
                                ins = dve.scalar_tensor_tensor(out=cacc[:, n, :], in0=cu[:, n, tap:tap + S],
                                                               scalar=col("conv_w_dw_2", KD * tap + n),
                                                               in1=cacc[:, n, :], op0=ALU.mult, op1=ALU.add)
                            if tap < WIDTH - 1:
                                step[n] = own(ins)
                            else:
                                ins.then_inc(conv_dve, 1)
                    dve.wait_ge(mean_done, MEAN_CONV)
                    for q in range(4):
                        dve.tensor_tensor(tmp[:, 2 * q:2 * q + 2, :], cacc[:, 2 * q:2 * q + 2, :],
                                          job_flat(w + 5, S).unsqueeze(1).to_broadcast([P, 2, S]), ALU.subtract)\
                            .then_inc(xc2_ready, 1)
                    iv = inverse()
                    normed(tmp, tmp, KD, xn_ready, iv)
                    act_high()
                    pieces(p + 20, p + 26)
                    post(g, w + 5)
                elif st["kind"] == "pool":
                    for _ in range(4):
                        dve.wait_ge(h_ready, k.next("h") + 1)
                    src, dst = ph, pa
                    step = None
                    for lv, win in enumerate(WINDOWS):
                        f = 2 * lv
                        if step is not None:
                            own_wait(step)
                        step = own(dve.tensor_tensor(dst[:, f:, win - 1:], src[:, f:, win - 1:],
                                                     src[:, f:, win - 1 - win // 2:PP - win // 2], ALU.add))
                        own_wait(step)
                        s, h = dst[:, f:f + 2, PADP:], ph[:, f:f + 2, PADP:]
                        dve.scalar_tensor_tensor(out=pp[:, f:f + 2, PADP:], in0=s[:, :, PADP:], scalar=1.0 / win,
                                                 in1=h[:, :, PADP:], op0=ALU.mult, op1=ALU.subtract)
                        own_wait(own(dve.tensor_tensor(pp[:, f:f + 2, 0:PADP], s[:, :, 0:PADP],
                                                       share[:, lv:lv + 1, :].to_broadcast([P, 2, PADP]), ALU.mult)))
                        own_wait(own(dve.tensor_tensor(pp[:, f:f + 2, 0:PADP], pp[:, f:f + 2, 0:PADP], h[:, :, 0:PADP],
                                                       ALU.subtract)))
                        dve.tensor_copy(a_hi[:, f:f + 2, :], pp[:, f:f + 2, :]).then_inc(pp_ready, 1)
                        src, dst = dst, (pb if dst is pa else pa)
                    for m in range(2):
                        dve.wait_ge(pool_done, m + 1)
                        for j in range(4):
                            f = 4 * m + j
                            ins = dve.tensor_scalar(tmp[:, f, :], job_banks(w + m)[:, j, :], col("pool_b_2", f),
                                                    col("pool_scale_2", f), ALU.add, ALU.mult)
                        ins.then_inc(bank_free[(w + m) % 2], 1)
                    post(g, w)
                elif st["kind"] == "ffn1":
                    def product(w, c, slot, n, i=0):
                        is_done(dve, c, i)
                        dve.wait_ge(sig_ready, n + 1)
                        dve.wait_ge(hid_ready, n + 1)
                        dve.tensor_tensor(ev[:, slot, :, :], sig[:, slot, :, :], job_banks(w)[:, 2:4, :], ALU.mult)\
                            .then_inc(bank_free[w % 2], 1)

                    n = st["hid"]

                    def two_jobs(i):
                        for b in range(2):
                            for h in range(2):
                                pieces(p + 4 + 4 * b + 2 * h, p + 6 + 4 * b + 2 * h, i)
                                mod_add(st["groups"][0], 2 * i + b, h)
                            product(w + b, c + 2 + 2 * b, b, n + 2 * i + b, i)

                    two_jobs(0)
                    with dve.Fori(1, 4) as i:
                        two_jobs(i)
                    for b in range(8, 11):
                        pieces(p + 4 * b + 4, p + 4 * b + 6)
                        if b == 8:
                            mod_finish(st["groups"][0], w + 9)
                        else:
                            mod_add(st["groups"][1], b - 9, 0)
                        pieces(p + 4 * b + 6, p + 4 * b + 8)
                        if b > 8:
                            mod_add(st["groups"][1], b - 9, 1)
                        product(w + b, c + 2 * b + 2, b % 2, n + b)
                    for m in range(2):
                        for u in range(6):
                            if m == 0 or u < 5:
                                pieces(p + 48 + 12 * m + 2 * u, p + 50 + 12 * m + 2 * u)
                            mod_add(st["groups"][1], 2 + (6 * m + u) // 2, u % 2)
                        residual(w + 11 + m, c + 28 + 6 * m, m, g)
                elif st["kind"] == "sb":
                    pieces(p + 4, p + 28)
                    for m in range(HEADS // 2 + 4):
                        if 2 <= m < HEADS // 2 + 2:
                            z = two(sb_z, m - 2)
                            dve.wait_ge(suf_done, m - 1)
                            dve.tensor_tensor(z, z, bk[:, 2:4, 0:384], ALU.subtract).then_inc(t_ready, 1)
                        if m < HEADS // 2:
                            z = two(sb_z, m)
                            dve.wait_ge(z_done, m + 1)
                            if m >= 3:
                                dve.wait_ge(e_ready, m - 2)
                            dve.tensor_scalar(z, bk[:, 6 * (m % 2):6 * (m % 2) + 2, 0:384], DH ** -0.5, None, ALU.mult)\
                                .then_inc(z_copied, 1)
                            dve.wait_ge(z_copied, m + 1)
                            dve.scalar_tensor_tensor(out=two(sb_l, m), in0=z, scalar=-1.0, in1=z,
                                                     op0=ALU.mult, op1=ALU.min).then_inc(n_ready, 1)
                        if 1 <= m <= HEADS // 2:
                            dve.wait_ge(l_ready, m)
                            dve.scalar_tensor_tensor(out=two(sb_s, m - 1), in0=two(sb_z, m - 1), scalar=0.0,
                                                     in1=two(sb_l, m - 1), op0=ALU.max, op1=ALU.add).then_inc(sp_ready, 1)
                            for h in range(2):
                                mod_add(st["groups"][0], m - 1, h)
                        heads_out(2 * (m - 4))
                    for m in range(2):
                        pieces(p + 28 + 4 * m, p + 32 + 2 * m)
                        residual(w + 6 + m, c + 14 + 2 * m, m, g)
                elif st["kind"] == "lru":
                    pieces(p + 4, p + 24)
                    step = {}
                    for a in range(0, NB, 2):
                        for tap in range(1, TAPS):
                            for n in range(a, a + 2):
                                if tap == 1:
                                    dve.wait_ge(xc_first, n + 1)
                                else:
                                    own_wait(step[n])
                                ins = dve.scalar_tensor_tensor(out=lxc[:, n, :], in0=lxb[:, n, tap:tap + S],
                                                               scalar=col("lru_conv_w", 10 * tap + n), in1=lxc[:, n, :],
                                                               op0=ALU.mult, op1=ALU.add)
                                if tap < TAPS - 1:
                                    step[n] = own(ins)
                                else:
                                    ins.then_inc(xc_ready, 1)
                    for n in range(NB):
                        dve.wait_ge(a_ready, n + 1)
                        step[n] = own(dve.tensor_tensor(lri[:, n, 0, :], lxb[:, n, 0:S], lxb[:, n, 0:S], ALU.mult))
                    for n in range(NB):
                        own_wait(step[n])
                        dve.scalar_tensor_tensor(out=lri[:, n, 0, :], in0=lri[:, n, 0, :], scalar=1.0,
                                                 in1=lru_t(n), op0=ALU.add, op1=ALU.mult).then_inc(v_ready, 1)
                    for n in range(NB):
                        dve.wait_ge(s_ready, n + 1)
                        dve.wait_ge(ix_ready, n + 1)
                        step[n] = own(dve.tensor_tensor(lri[:, n, 1, :], lri[:, n, 0, :], lri[:, n, 1, :], ALU.mult))
                    for n in range(NB):
                        own_wait(step[n])
                        step[n] = own(dve.tensor_tensor_scan(lxc[:, n, :], lxb[:, n, 0:S], lri[:, n, 1, :], 0.0,
                                                             ALU.mult, ALU.add))
                    for n in range(NB):
                        own_wait(step[n])
                        step[n] = own(dve.tensor_tensor(lg[:, n, :], lg[:, n, :], lxc[:, n, :], ALU.mult))
                    for n in range(NB):
                        own_wait(step[n])
                        dve.tensor_copy(y_hi(n), lg[:, n, :]).then_inc(y_ready, 1)
                    for m in range(2):
                        pieces(p + 24 + 6 * m, p + 30 + 4 * m)
                        residual(w + 5 + m, c + 13 + 3 * m, m, g)

            if len(stages) <= 6:
                final_norm()
            for b in range(2):
                dve.wait_ge(turn_done, k.next("turn") + 1)
                ins = dve.tensor_copy(oout[:, b, :], job_flat(W_END + b, D))
            ins.then_inc(out_ready, 1)


_INS = ["x", "c", "mod_w", "mod_b", "norm_g", "ffn_w_gu", "ffn_w_down", "sb_w_qkv", "sb_w_o", "lru_w_in",
        "lru_conv_w", "lru_conv_b", "lru_w_r", "lru_b_r", "lru_w_i", "lru_b_i", "lru_lambda", "lru_w_out",
        "final_norm_g", "c_2", "positions_2", "ada_w_2", "ada_b_2", "norm_g_2", "mla_w_dq_2", "mla_q_norm_g_2",
        "mla_w_uq_2", "mla_w_dkv_2", "mla_kv_norm_g_2", "mla_w_ukv_2", "mla_w_o_2", "conv_w_pw1_2",
        "conv_b_pw1_2", "conv_w_dw_2", "conv_b_dw_2", "conv_ln_g_2", "conv_ln_b_2", "conv_w_pw2_2",
        "conv_b_pw2_2", "pool_w_2", "pool_b_2", "pool_scale_2", "ffn_w1_2", "ffn_w2_2"]


def kernel(**inputs):
    import concourse.bacc as bacc
    from concourse.bass_utils import run_bass_kernel_spmd

    nc = bacc.Bacc("TRN2", target_bir_lowering=False, num_devices=1)
    arrays, tensors = {}, {}
    for name in _INS:
        a = np.ascontiguousarray(inputs[name])
        arrays[f"in_{name}"] = a
        tensors[name] = nc.dram_tensor(f"in_{name}", a.shape, mybir.dt.from_np(a.dtype), kind="ExternalInput").ap()
    out = nc.dram_tensor("out", (1, S, D), F32, kind="ExternalOutput").ap()
    build(nc, tensors, out)
    got = run_bass_kernel_spmd(nc, [arrays], core_ids=[0])
    return got.results[0]["out"]
```
